# Optimizing a Trainium2 kernel written in Bass

```python
import math
import jax, jax.numpy as jnp
from jax import lax
import numpy as np

D_MODEL = 2048
BATCH = 1
SEQ = 256
DEPTH = 2
DEC_BATCH = 8
DEC_SEQ = 8
PAST_LEN = 2048
PAGE_SIZE = 128

CHUNK = 128
N_HEADS_A = 8
HEAD_DIM_A = 128
W_A = N_HEADS_A * HEAD_DIM_A
N_GROUPS_B = 8
W_B = D_MODEL - W_A
CONV_W = 3
D_FF = 5632
N_MOD = 6
IN_COLS = 2 * W_A + 3 * W_B
EPS = 1e-6

kernel_name = "hymba_style_gmlp_shortconv_convffn_step"

def rmsnorm(x, g):
    xf = x.astype(jnp.float32)
    y = xf * lax.rsqrt(jnp.mean(xf * xf, axis=-1, keepdims=True) + EPS)
    return (y * g.astype(jnp.float32)).astype(x.dtype)

def causal_conv3(x, past, w, b=None):
    xp = jnp.concatenate([past.astype(x.dtype), x], axis=1)
    y = w[0] * xp[:, :-2] + w[1] * xp[:, 1:-1] + w[2] * xp[:, 2:]
    if b is not None:
        y = y + b
    return y, xp[:, -(CONV_W - 1):]

def chunk_spatial_gate(z, g_v, w_s, b_s):
    bsz, t_len, _ = z.shape
    u, v = z[..., :W_A], z[..., W_A:]
    v = rmsnorm(v, g_v)
    blk = CHUNK if t_len >= CHUNK else t_len
    n_c = -(-t_len // blk)
    t_pad = n_c * blk
    vp = jnp.pad(v, ((0, 0), (0, t_pad - t_len), (0, 0)))
    vp = vp.reshape(bsz, n_c, blk, N_HEADS_A, HEAD_DIM_A)
    mask = jnp.tril(jnp.ones((blk, blk), dtype=bool))
    w = jnp.where(mask[None], w_s[:, :blk, :blk], jnp.zeros((), w_s.dtype))
    mixed = jnp.einsum('hts,bnshd->bnthd', w, vp)
    mixed = mixed + jnp.transpose(b_s[:, :blk])[None, None, :, :, None]
    mixed = mixed.reshape(bsz, t_pad, W_A)[:, :t_len]
    start = ((t_len - 1) // CHUNK) * CHUNK
    return u * mixed, v[:, start:]

def layer(x, c, past_mix, past_ffn, w_ada, b_ada, g_pre_mix, g_post_mix, g_pre_ffn, g_post_ffn,
          w_in, g_v, w_spatial, b_spatial, w_conv_mix, g_out_a, g_out_b, w_out,
          w_up, w_conv_ffn, b_conv_ffn, w_down):
    mod = jax.nn.silu(c) @ w_ada + b_ada
    sh1, sc1, gt1, sh2, sc2, gt2 = jnp.split(mod[:, None, :], N_MOD, axis=-1)

    h = rmsnorm(x, g_pre_mix) * (1 + sc1) + sh1
    proj = h @ w_in
    z_a = proj[..., :2 * W_A]
    gate_b = proj[..., 2 * W_A:2 * W_A + W_B]
    gate_c = proj[..., 2 * W_A + W_B:2 * W_A + 2 * W_B]
    h_b = proj[..., 2 * W_A + 2 * W_B:]
    out_a, v_rows = chunk_spatial_gate(jax.nn.gelu(z_a), g_v, w_spatial, b_spatial)
    conv_out, new_mix = causal_conv3(gate_c * h_b, past_mix, w_conv_mix)
    out_b = gate_b * conv_out
    merged = jnp.concatenate([rmsnorm(out_a, g_out_a), rmsnorm(out_b, g_out_b)], axis=-1) @ w_out
    x = x + gt1 * rmsnorm(merged, g_post_mix)

    h = rmsnorm(x, g_pre_ffn) * (1 + sc2) + sh2
    up = h @ w_up
    up_c, new_ffn = causal_conv3(up, past_ffn, w_conv_ffn, b_conv_ffn)
    ff = (jax.nn.silu(up_c[..., :D_FF]) * up_c[..., D_FF:]) @ w_down
    x = x + gt2 * rmsnorm(ff, g_post_ffn)
    return x, new_mix, new_ffn, v_rows

def run_trunk(x, c, past_mix, past_ffn, w_ada, b_ada, g_pre_mix, g_post_mix, g_pre_ffn, g_post_ffn,
              w_in, g_v, w_spatial, b_spatial, w_conv_mix, g_out_a, g_out_b, w_out,
              w_up, w_conv_ffn, b_conv_ffn, w_down):
    mixes, ffns, vrows = [], [], []
    for l in range(DEPTH):
        x, nm, nf, vr = layer(x, c, past_mix[:, l], past_ffn[:, l], w_ada[l], b_ada[l],
                              g_pre_mix[l], g_post_mix[l], g_pre_ffn[l], g_post_ffn[l],
                              w_in[l], g_v[l], w_spatial[l], b_spatial[l], w_conv_mix[l],
                              g_out_a[l], g_out_b[l], w_out[l],
                              w_up[l], w_conv_ffn[l], b_conv_ffn[l], w_down[l])
        mixes.append(nm)
        ffns.append(nf)
        vrows.append(vr)
    return x, jnp.stack(mixes, axis=1), jnp.stack(ffns, axis=1), jnp.stack(vrows, axis=1)

def setup_inputs(seed: int = 0) -> dict:
    key = jax.random.key(seed)
    ks = jax.random.split(key, 26)
    f32 = jnp.float32
    nrm = lambda k, shape, s: jax.random.normal(k, shape, f32) * s
    gain = lambda k, shape: 1.0 + 0.05 * jax.random.normal(k, shape, f32)
    return {
        "x_prompt": nrm(ks[0], (BATCH, SEQ, D_MODEL), 1.0),
        "x_sample": nrm(ks[1], (DEC_BATCH, DEC_SEQ, D_MODEL), 1.0),
        "state_conv_mix": nrm(ks[2], (DEC_BATCH, DEPTH, CONV_W - 1, W_B), 1.0),
        "state_conv_ffn": nrm(ks[3], (DEC_BATCH, DEPTH, CONV_W - 1, 2 * D_FF), 1.0),
        "c_prompt": nrm(ks[4], (BATCH, D_MODEL), 1.0),
        "c_sample": nrm(ks[5], (DEC_BATCH, D_MODEL), 1.0),
        "w_ada": nrm(ks[6], (DEPTH, D_MODEL, N_MOD * D_MODEL), 0.5 * D_MODEL ** -0.5),
        "b_ada": nrm(ks[7], (DEPTH, N_MOD * D_MODEL), 0.02),
        "g_pre_mix": gain(ks[8], (DEPTH, D_MODEL)),
        "g_post_mix": gain(ks[9], (DEPTH, D_MODEL)),
        "g_pre_ffn": gain(ks[10], (DEPTH, D_MODEL)),
        "g_post_ffn": gain(ks[11], (DEPTH, D_MODEL)),
        "w_in": nrm(ks[12], (DEPTH, D_MODEL, IN_COLS), D_MODEL ** -0.5),
        "g_v": gain(ks[13], (DEPTH, W_A)),
        "w_spatial": nrm(ks[14], (DEPTH, N_HEADS_A, CHUNK, CHUNK), 0.5 * CHUNK ** -0.5),
        "b_spatial": 1.0 + nrm(ks[15], (DEPTH, N_HEADS_A, CHUNK), 0.02),
        "w_conv_mix": nrm(ks[16], (DEPTH, CONV_W, W_B), CONV_W ** -0.5),
        "g_out_a": gain(ks[17], (DEPTH, W_A)),
        "g_out_b": gain(ks[18], (DEPTH, W_B)),
        "w_out": nrm(ks[19], (DEPTH, W_A + W_B, D_MODEL), (W_A + W_B) ** -0.5),
        "w_up": nrm(ks[20], (DEPTH, D_MODEL, 2 * D_FF), D_MODEL ** -0.5),
        "w_conv_ffn": nrm(ks[21], (DEPTH, CONV_W, 2 * D_FF), CONV_W ** -0.5),
        "b_conv_ffn": nrm(ks[22], (DEPTH, 2 * D_FF), 0.02),
        "w_down": nrm(ks[23], (DEPTH, D_FF, D_MODEL), D_FF ** -0.5),
    }

def reference(x_prompt, x_sample, state_conv_mix, state_conv_ffn, c_prompt, c_sample,
              w_ada, b_ada, g_pre_mix, g_post_mix, g_pre_ffn, g_post_ffn,
              w_in, g_v, w_spatial, b_spatial, w_conv_mix, g_out_a, g_out_b, w_out,
              w_up, w_conv_ffn, b_conv_ffn, w_down):
    weights = (w_ada, b_ada, g_pre_mix, g_post_mix, g_pre_ffn, g_post_ffn,
               w_in, g_v, w_spatial, b_spatial, w_conv_mix, g_out_a, g_out_b, w_out,
               w_up, w_conv_ffn, b_conv_ffn, w_down)
    bp = x_prompt.shape[0]
    zero_mix = jnp.zeros((bp, DEPTH, CONV_W - 1, W_B), x_prompt.dtype)
    zero_ffn = jnp.zeros((bp, DEPTH, CONV_W - 1, 2 * D_FF), x_prompt.dtype)
    y_prompt, mix_p, ffn_p, vrows_p = run_trunk(x_prompt, c_prompt, zero_mix, zero_ffn, *weights)
    y_sample, mix_s, ffn_s, vrows_s = run_trunk(x_sample, c_sample, state_conv_mix, state_conv_ffn, *weights)
    return (y_prompt, y_sample, mix_p, mix_s, ffn_p, ffn_s, vrows_p, vrows_s)


_drawn_inputs = setup_inputs


def setup_inputs(seed=0):
    import zlib

    import numpy as np

    out = dict(_drawn_inputs(seed))
    spreads = {}
    factors = {'g_post_mix': 2.688,
     'g_post_ffn': 2.929,
     'b_spatial': 8.0,
     'g_out_a': 3.881,
     'g_out_b': 3.955,
     'b_conv_ffn': 5.479}
    for name, (base, spread) in spreads.items():
        noise = np.random.default_rng([zlib.crc32(name.encode()), seed]).standard_normal(out[name].shape)
        drawn = base * np.exp(spread * noise) if base else spread * noise
        out[name] = __import__('jax').numpy.asarray(drawn.astype(out[name].dtype))
    for name, factor in factors.items():
        out[name] = (out[name] * factor).astype(out[name].dtype)
    return out
```

```python
from contextlib import ExitStack

import concourse.bass as bass
from concourse import mybir

F32 = mybir.dt.float32
F32R = mybir.dt.float32r
ALU = mybir.AluOpType
ACT = mybir.ActivationFunctionType

P = 128
DEPTH = 2
D_MODEL = 2048
SEQ = 256
SEQS = 8
STEP = 8
W_A = 1024
W_B = 1024
D_FF = 5632
EPS = 1e-6

T = SEQ + SEQS * STEP
R = 1 + SEQS
KD = D_MODEL // P
HA = W_A // P
HB = W_B // P
PAD = 2 + SEQ + SEQS * (2 + STEP)
CONV = PAD - 2
SROW = 2 + STEP
S0 = 2 + SEQ
G = D_FF // (4 * P)

UNIT = 2048
RAW = 4
SPLIT = 2
A_UNITS = 2 * HA + 3 * HB + KD
UNITS = A_UNITS + G * 12
A_BLOCKS = A_UNITS
BLOCKS = A_BLOCKS + G * (8 + KD)
ADA_CHUNKS = 6 * D_MODEL // 512
ADA_TOTAL = DEPTH * ADA_CHUNKS
ADA_AHEAD = 8
ADA_A = A_UNITS // 4
SHIFT1, SCALE1, GATE1, SHIFT2, SCALE2, GATE2 = range(6)

G_PRE_MIX, G_POST_MIX, G_PRE_FFN, G_POST_FFN = 0, KD, 2 * KD, 3 * KD
G_V = 4 * KD
G_OUT = G_V + HA
W_MIX = G_OUT + KD
W_CF = W_MIX + 3 * HB
NPAR = W_CF + 4 * 8 * G

CHAINS = 6
SQUARES = HA + HB + HA + KD + KD
PADS = HB + 8 * G


def trunk_kernel(nc, x_t, c_t, consts, params, b_ada_t, mix_hist, ffn_hist, w_sp, w_sp_s, b_sp, ada_units,
                 w_units, y_t, new_mix, new_ffn, v_rows):
    with ExitStack() as ctx:
        at = [(nc.sbuf_base + 63) // 64 * 64]

        def place(name, shape, dtype=F32, offset=None):
            size = 4
            for n in shape[1:]:
                size *= n
            here = at[0] if offset is None else offset
            tensor = nc.alloc_sbuf_tensor_at(name, shape, dtype, offset=here)
            if offset is None:
                at[0] += (size + 31) // 32 * 32
            return tensor, here + (size + 31) // 32 * 32

        def sb(name, shape, dtype=F32):
            return place(name, shape, dtype)[0]

        def sem(name):
            return ctx.enter_context(nc.semaphore(name))

        x = sb("x", [P, KD, T])
        h_hi = sb("h_hi", [P, KD, T], F32R)
        h_lo = sb("h_lo", [P, KD, T], F32R)
        w_raw = sb("w_raw", [P, RAW, UNIT])
        w_hi = sb("w_hi", [P, SPLIT, UNIT], F32R)
        w_lo = sb("w_lo", [P, SPLIT, UNIT], F32R)
        ada_raw = sb("ada_raw", [P, 2, 4, 512])
        stage = sb("stage", [P, KD, T])
        mod = sb("mod", [P, DEPTH * 6 * KD, R])
        pad = sb("pad", [P, 2, PAD])
        ada_sum = sb("ada_sum", [P, 512])
        sq_sum = sb("sq_sum", [P, 2, T])
        sq = sb("sq", [P, T])
        diag = sb("diag", [P, 2, T])
        par = sb("par", [P, DEPTH * NPAR])
        b_ada = sb("b_ada", [P, DEPTH * 6 * KD])
        coef_scale = sb("coef_scale", [P, KD, R])
        coef_shift = sb("coef_shift", [P, KD, R])
        coef_gate = sb("coef_gate", [P, KD, R])
        c_act = sb("c_act", [P, KD, 32])
        cst = sb("cst", [P, P + R])
        ones = sb("ones", [P, P])
        mix_new = sb("mix_new", [P, HB, R, 2])
        mix_old = sb("mix_old", [P, HB, SEQS, 2])
        var = sb("var", [P, 6])
        rstd = sb("rstd", [P, 6])
        minus_half = sb("minus_half", [P, 6])
        warm = sb("warm", [P, 2])
        ident = cst[:, 0:P]
        select = cst[:, P:P + R]

        zone = at[0]
        c_raw, _ = place("c_raw", [P, KD, R], F32, zone)
        v_norm, e = place("v_norm", [P, 2, T], F32, zone)
        v_tok, e = place("v_tok", [P, 2, 3 * P], F32, e)
        sp_w, e = place("sp_w", [P, HA * P], F32, e)
        sp_ws, e = place("sp_ws", [SEQS * STEP, HA * SEQS * STEP], F32, e)
        sp_b, e = place("sp_b", [1, HA * P], F32, e)
        gate_c, e = place("gate_c", [P, T], F32, e)
        conv_mix, e = place("conv_mix", [P, CONV], F32, e)
        u_act, end_mix = place("u_act", [P, T], F32, e)
        ff_hi, e = place("ff_hi", [P, 4, T], F32R, zone)
        ff_lo, e = place("ff_lo", [P, 4, T], F32R, e)
        ffn_old, e = place("ffn_old", [P, 8, SEQS, 2], F32, e)
        ffn_new, e = place("ffn_new", [P, 8, R, 2], F32, e)
        conv_ffn, e = place("conv_ffn", [P, 2, CONV], F32, e)
        gate_act, e = place("gate_act", [P, CONV], F32, e)
        ff, end_ffn = place("ff", [P, T], F32, e)
        assert max(end_mix, end_ffn) <= nc.sbuf_usable_end, (end_mix, end_ffn, nc.sbuf_usable_end)

        main = [ctx.enter_context(nc.psum_tensor(f"main{i}", [P, 512], F32)) for i in range(2)]
        ada_acc = ctx.enter_context(nc.psum_tensor("ada_acc", [P, 512], F32))
        ada_turn_acc = ctx.enter_context(nc.psum_tensor("ada_turn_acc", [P, 512], F32))
        rb = [ctx.enter_context(nc.psum_tensor(f"rb{i}", [P, 512], F32)) for i in range(2)]
        tok = ctx.enter_context(nc.psum_tensor("tok", [P, 512], F32))
        mixed = ctx.enter_context(nc.psum_tensor("mixed", [P, 512], F32))
        ada_t = ada_turn_acc[:, 0:4 * R].rearrange("p (b r) -> p b r", r=R)
        stat = tok[:, 3 * P:3 * P + 6]

        loaded = sem("loaded")
        w_landed = [sem(f"w_landed{i}") for i in range(RAW)]
        ada_landed = [sem(f"ada_landed{i}") for i in range(2)]
        mix_landed = sem("mix_landed")
        hist_landed = sem("hist_landed")
        v_saved = [sem(f"v_saved{i}") for i in range(2)]
        mix_saved = sem("mix_saved")
        ffn_saved = sem("ffn_saved")
        y_saved = sem("y_saved")
        made = sem("made")
        c_ready = sem("c_ready")
        hi_done = sem("hi_done")
        split_done = sem("split_done")
        blocks_done = sem("blocks_done")
        taken = [sem(f"taken{i}") for i in range(2)]
        ada_used = sem("ada_used")
        ada_out = sem("ada_out")
        ada_turned = sem("ada_turned")
        mod_ready = sem("mod_ready")
        coef_ready = sem("coef_ready")
        sq_reset = sem("sq_reset")
        sq_one = sem("sq_one")
        sq_added = sem("sq_added")
        norm_sum = sem("norm_sum")
        norm_var = sem("norm_var")
        norm_rstd = sem("norm_rstd")
        norm_diag = sem("norm_diag")
        norm_rb = sem("norm_rb")
        post_scaled = sem("post_scaled")
        post_sample = sem("post_sample")
        x_prompt = sem("x_prompt")
        x_sample = sem("x_sample")
        x_squares = sem("x_squares")
        x_scaled = sem("x_scaled")
        h_prompt = sem("h_prompt")
        h_sample = sem("h_sample")
        ab_scaled = sem("ab_scaled")
        hi_h = sem("hi_h")
        h_ready = sem("h_ready")
        masked = sem("masked")
        v_normed = sem("v_normed")
        v_free = sem("v_free")
        v_turned = sem("v_turned")
        v_tokens = sem("v_tokens")
        mix_done = sem("mix_done")
        mixed_out = sem("mixed_out")
        a_ready = sem("a_ready")
        pad_hist = sem("pad_hist")
        pad_kept = sem("pad_kept")
        tap2 = sem("tap2")
        tap1 = sem("tap1")
        conv_done = sem("conv_done")
        gate_done = sem("gate_done")
        ff_done = sem("ff_done")
        ff_hi_done = sem("ff_hi_done")
        ff_ready = sem("ff_ready")
        zeroed = sem("zeroed")
        passed = sem("passed")

        def within(index, n):
            return nc.s_assert_within(index, 0, n - 1, skip_runtime_bounds_check_because="an If checks it")

        def pcol(l, column):
            return par[:, bass.ds(l * NPAR + column, 1)]

        def samples(row):
            return row[:, SEQ:T].rearrange("p (s t) -> p s t", t=STEP)

        def padded(row, first, n):
            return row[:, S0:PAD].rearrange("p (s t) -> p s t", t=SROW)[:, :, first:first + n]

        def conv_samples(row):
            return row[:, SEQ:CONV].rearrange("p (s t) -> p s t", t=SROW)[:, :, 2:SROW]

        def quarter_samples(t, q):
            return t[:, 4 * q:4 * q + 4, SEQ:T].rearrange("p b (s t) -> p b s t", t=STEP)

        def per_sample(coef, q):
            return coef[:, 4 * q:4 * q + 4, 1:R].unsqueeze(3).broadcast_to([P, 4, SEQS, STEP])

        def over_blocks(bank, n):
            return bank[:, 0:T].unsqueeze(1).broadcast_to([P, n, T])

        def apart(eng):
            eng.sem_inc(passed, 1)

        block = ctx.enter_context(nc.Block())

        @block.sync
        def _(sp):
            def load_w(u, slot):
                sp.wait_ge(split_done, u + 1)
                sp.dma_start(w_raw[:, slot, :], w_units[u]).then_inc(w_landed[slot], 16)

            def load_ada(a, slot, first=False):
                if not first:
                    sp.wait_ge(ada_used, a - 1)
                sp.dma_start(ada_raw[:, slot, :, :], ada_units[a]).then_inc(ada_landed[slot], 16)

            for a in range(2):
                load_ada(a, a, first=True)
            with sp.Fori(1, 2 * ADA_AHEAD) as pair:
                for j in range(2):
                    load_ada(2 * pair + j, j)
            with sp.Fori(0, DEPTH) as l:
                w0 = UNITS * l
                a0 = 4 * (ADA_AHEAD + ADA_CHUNKS * l)
                for u in range(2):
                    load_w(w0 + u, u)
                with sp.Fori(0, ADA_A - 1) as i:
                    for j in range(4):
                        load_w(w0 + 4 * i + 2 + j, (2 + j) % RAW)
                        load_ada(a0 + 4 * i + j, j % 2)
                for j in range(4):
                    load_w(w0 + A_UNITS - 2 + j, (2 + j) % RAW)
                    if j != 1:
                        load_ada(a0 + 4 * ADA_A - 4 + j - (j > 1), (j - (j > 1)) % 2)
                load_ada(a0 + 4 * ADA_A - 1, 1)
                for u in range(2, 8):
                    load_w(w0 + A_UNITS + u, u % RAW)
                with sp.Fori(0, G - 1) as g:
                    for part in range(3):
                        for j in range(4):
                            load_w(w0 + A_UNITS + 8 + 12 * g + 4 * part + j, j)
                        if part < 2:
                            with sp.If(ADA_AHEAD + ADA_CHUNKS * l + ADA_A + g < ADA_TOTAL):
                                for j in range(2):
                                    a = within(a0 + 4 * ADA_A + 4 * g + 2 * part + j, 4 * ADA_TOTAL)
                                    load_ada(a, j)
                for j in range(4):
                    load_w(w0 + UNITS - 4 + j, j)
            sp.wait_ge(x_prompt, 4 + 8 * DEPTH)
            sp.wait_ge(x_sample, 4 + 8 * DEPTH)
            sp.dma_start(y_t, x[:, :, :]).then_inc(y_saved, 16)
            sp.wait_ge(y_saved, 16)
            for s in v_saved:
                sp.wait_ge(s, 16 * (DEPTH * HA // 2))
            sp.wait_ge(mix_saved, 16 * DEPTH)
            sp.wait_ge(ffn_saved, 16 * DEPTH * G)

        @block.gpsimd
        def _(pool):
            pool.memset(ones[:, :], 1.0).then_inc(made, 1)
            pool.memset(minus_half[:, :], -0.5).then_inc(made, 1)
            pool.memset(c_act[:, :, :], 0.0).then_inc(made, 1)
            pool.memset(pad[:, :, 0:2], 0.0).then_inc(made, 1)
            pool.sem_inc(v_free, 2)
            pool.sem_inc(sq_added, 1)
            pool.sem_inc(pad_kept, 2)
            pool.sem_inc(x_sample, 4)

            def reset_sums(n):
                pool.memset(sq_sum[:, :, :], 0.0).then_inc(sq_reset, 1)
                pool.wait_ge(sq_reset, n)
                apart(pool)

            def add_square(l, k, source, which):
                pool.wait_ge(sq_added, SQUARES * l + k + 1)
                pool.tensor_tensor(sq[:, :], source, source, ALU.mult).then_inc(sq_one, 1)
                pool.wait_ge(sq_one, SQUARES * l + k + 1)
                pool.tensor_tensor(sq_sum[:, which, :], sq_sum[:, which, :], sq[:, :], ALU.add)\
                    .then_inc(sq_added, 1)

            def root(l, k, n):
                pool.wait_ge(norm_var, CHAINS * l + k + 1)
                pool.tensor_tensor(rstd[:, 0:n], var[:, 0:n], minus_half[:, 0:n], ALU.pow)\
                    .then_inc(norm_rstd, 1)

            def fill_history(w, slot, source):
                pool.wait_ge(conv_done, w + 1)
                apart(pool)
                pool.tensor_copy(padded(pad[:, slot, :], 0, 2), source).then_inc(pad_hist, 1)

            def keep_last(slot, target):
                apart(pool)
                pool.tensor_copy(target[:, 0, :], pad[:, slot, SEQ:S0])
                pool.tensor_copy(target[:, 1:R, :], padded(pad[:, slot, :], STEP, 2)).then_inc(pad_kept, 1)

            def load_history(l, g):
                pool.dma_start(ffn_old[:, :, :, :].rearrange("p b s t -> p (b s t)"), ffn_hist[l, g])\
                    .then_inc(hist_landed, 16)

            def sample_update(l, e):
                pool.wait_ge(coef_ready, 4 * l + 2 * e + 2)
                for q in range(4):
                    n = 8 * l + 4 * e + q
                    pool.wait_ge(post_scaled, n + 1)
                    pool.tensor_tensor(quarter_samples(stage, q), quarter_samples(stage, q),
                                       per_sample(coef_gate, q), ALU.mult).then_inc(post_sample, 1)
                    pool.wait_ge(post_sample, n + 1)
                    pool.tensor_tensor(quarter_samples(x, q), quarter_samples(x, q),
                                       quarter_samples(stage, q), ALU.add).then_inc(x_sample, 1)

            def modulate_samples(l, e):
                pool.wait_ge(coef_ready, 4 * l + 2 * e + 1)
                for q in range(4):
                    n = 8 * l + 4 * e + q
                    pool.wait_ge(x_scaled, n + 1)
                    pool.tensor_tensor(quarter_samples(stage, q), quarter_samples(stage, q),
                                       per_sample(coef_scale, q), ALU.mult).then_inc(h_sample, 1)
                    pool.wait_ge(h_sample, 2 * n + 1)
                    pool.tensor_tensor(quarter_samples(stage, q), quarter_samples(stage, q),
                                       per_sample(coef_shift, q), ALU.add).then_inc(h_sample, 1)

            pool.wait_ge(made, 4)
            with pool.Fori(0, DEPTH) as l:
                b0 = BLOCKS * l
                pool.wait_ge(blocks_done, b0 + 1)
                pool.wait_ge(c_ready, 1)
                pool.dma_start(sp_w[:, :], w_sp[l]).then_inc(mix_landed, 16)
                pool.dma_start(sp_ws[:, :], w_sp_s[l]).then_inc(mix_landed, 16)
                pool.dma_start(sp_b[0:1, :], b_sp[l]).then_inc(mix_landed, 16)
                pool.dma_start(mix_old[:, :, :, :].rearrange("p b s t -> p (b s t)"), mix_hist[l])\
                    .then_inc(mix_landed, 16)
                root(l, 0, 3)
                modulate_samples(l, 0)
                pool.wait_ge(mix_landed, 64 * l + 64)
                apart(pool)
                wp = sp_w[:, :].rearrange("p (h t) -> p h t", t=P)
                pool.affine_select(out=wp, in_=wp, compare_op=ALU.is_ge, fill=0.0, base=0,
                                   pattern=[[0, HA], [1, P]], channel_multiplier=-1).then_inc(masked, 1)
                ws = sp_ws[:, :].rearrange("p (h t) -> p h t", h=HA)
                pool.affine_select(out=ws, in_=ws, compare_op=ALU.is_ge, fill=0.0, base=0,
                                   pattern=[[0, HA], [1, SEQS * STEP]], channel_multiplier=-1)\
                    .then_inc(masked, 1)
                reset_sums(4 * l + 1)
                with pool.Fori(0, HA // 4) as i:
                    for jj in range(4):
                        pool.wait_ge(taken[jj % 2], BLOCKS // 2 * l + 2 * i + jj // 2 + 2)
                        add_square(l, 4 * i + jj, stage[:, 4 * i + jj, :], 0)
                root(l, 1, 3)
                reset_sums(4 * l + 2)
                with pool.Fori(0, HB // 4) as i:
                    for jj in range(4):
                        j = 4 * i + jj
                        w = PADS * l + j
                        fill_history(w, jj % 2, mix_old[:, j, :, :])
                        pool.wait_ge(v_normed, HA * l + j + 1)
                        pool.dma_start(v_rows[l, j], v_norm[:, jj % 2, P:T]).then_inc(v_saved[jj % 2], 16)
                        bh = HA + 3 * jj + 1
                        pool.wait_ge(taken[bh % 2], BLOCKS // 2 * l + 6 * i + bh // 2 + 2)
                        keep_last(jj % 2, mix_new[:, j, :, :])
                        bb = bh + 1
                        pool.wait_ge(taken[bb % 2], BLOCKS // 2 * l + 6 * i + bb // 2 + 2)
                        add_square(l, HA + j, stage[:, HA + j, :], 1)
                        pool.wait_ge(v_saved[jj % 2], 16 * (HA // 2 * l + 2 * i + jj // 2 + 1))
                        pool.sem_inc(v_free, 1)
                pool.wait_ge(pad_kept, PADS * l + HB + 2)
                pool.dma_start(new_mix[l], mix_new[:, :, :, :].rearrange("p b s t -> p (b s t)"))\
                    .then_inc(mix_saved, 16)
                with pool.Fori(0, HA // 4) as i:
                    for jj in range(4):
                        j = 4 * i + jj
                        pool.wait_ge(a_ready, HA * l + j + 2)
                        add_square(l, HA + HB + j, stage[:, j, :], 0)
                root(l, 2, 6)
                pool.wait_ge(mix_saved, 16 * l + 16)
                pool.wait_ge(a_ready, HA * l + HA + 1)
                load_history(l, 0)
                reset_sums(4 * l + 3)
                with pool.Fori(0, KD // 4) as i:
                    for jj in range(4):
                        b = A_UNITS - KD + jj
                        pool.wait_ge(taken[b % 2], BLOCKS // 2 * l + 2 * i + b // 2 + 2)
                        add_square(l, 2 * HA + HB + 4 * i + jj, stage[:, 4 * i + jj, :], 0)
                root(l, 3, 3)
                sample_update(l, 0)
                root(l, 4, 3)
                modulate_samples(l, 1)
                pool.wait_ge(h_ready, 12 * l + 12)
                apart(pool)
                pool.memset(stage[:, :, :], 0.0).then_inc(zeroed, 1)
                reset_sums(4 * l + 4)

                def group_states(l, g, half, first=False, last=False):
                    pool.wait_ge(hist_landed, 16 * (G * l + g + 1))
                    for n in range(8):
                        w = PADS * l + HB + 8 * g + n
                        fill_history(w, n % 2, ffn_old[:, n, :, :])
                        if n == 7 and not last:
                            pool.wait_ge(pad_hist, w + 1)
                            load_history(l, g + 1)
                        if n == 0 and not first:
                            pool.wait_ge(ffn_saved, 16 * (G * l + g))
                        pool.wait_ge(taken[n % 2], BLOCKS // 2 * l + half(n) + 2)
                        keep_last(n % 2, ffn_new[:, n, :, :])
                    pool.wait_ge(pad_kept, PADS * l + HB + 8 * g + 10)
                    pool.dma_start(new_ffn[l, g], ffn_new[:, :, :, :].rearrange("p b s t -> p (b s t)"))\
                        .then_inc(ffn_saved, 16)

                def half_block(g):
                    first = A_BLOCKS // 2 + 4 + (4 + KD // 2) * (g - 1)
                    return lambda n: first + (n if n < 2 else n + KD) // 2

                group_states(l, 0, lambda n: (A_BLOCKS + n) // 2, first=True)
                with pool.Fori(1, G - 1) as g:
                    group_states(l, g, half_block(g))
                group_states(l, G - 1, half_block(G - 1), last=True)
                with pool.Fori(0, KD // 4) as i:
                    for jj in range(4):
                        b = BLOCKS - KD + jj
                        pool.wait_ge(taken[b % 2], BLOCKS // 2 * l + 2 * i + b // 2 + 2)
                        add_square(l, SQUARES - KD + 4 * i + jj, stage[:, 4 * i + jj, :], 0)
                root(l, 5, 3)
                sample_update(l, 1)
                pool.wait_ge(ffn_saved, 16 * G * (l + 1))
                apart(pool)

        @block.tensor
        def _(pe):
            pe.sem_inc(blocks_done, 1)
            pe.sem_inc(ada_turned, 1)

            def split_ready(u):
                pe.wait_ge(split_done, RAW + u + 1)

            def bank_free(l, half, bank):
                pe.wait_ge(taken[bank], BLOCKS // 2 * l + half + 1)

            def three(out, hi, lo, k, moving_hi, moving_lo, first, last):
                pe.matmul(out, hi, moving_hi[:, k, :], start=first, stop=False)
                pe.matmul(out, hi, moving_lo[:, k, :], start=False, stop=False)
                return pe.matmul(out, lo, moving_hi[:, k, :], start=False, stop=last)

            def unit_block(l, u, half, slot, bank, h_from=None):
                split_ready(UNITS * l + u)
                bank_free(l, half, bank)
                for k in range(KD):
                    if h_from is not None and k % 4 == 0:
                        pe.wait_ge(h_ready, h_from + k // 4 + 1)
                    cols = slice(k * P, (k + 1) * P)
                    mm = three(main[bank][:, 0:T], w_hi[:, slot, cols], w_lo[:, slot, cols], k, h_hi, h_lo,
                               k == 0, k == KD - 1)
                mm.then_inc(blocks_done, 1)

            def down_unit(l, u, half, slot):
                split_ready(UNITS * l + u)
                for m in range(4):
                    bank_free(l, half + m // 2, m % 2)
                    for k in range(4):
                        cols = slice(k * 512 + m * P, k * 512 + (m + 1) * P)
                        mm = three(main[m % 2][:, 0:T], w_hi[:, slot, cols], w_lo[:, slot, cols], k, ff_hi,
                                   ff_lo, k == 0, k == 3)
                    mm.then_inc(blocks_done, 1)

            def ada_part(c, parts):
                for kk in parts:
                    if kk == 0:
                        pe.wait_ge(ada_out, c + 1)
                    pe.wait_ge(ada_landed[kk % 2], 16 * (2 * c + kk // 2 + 1))
                    for j in range(4):
                        mm = pe.matmul(ada_acc[32 * j:32 * j + 32, :], c_act[:, 4 * kk + j, :],
                                       ada_raw[:, kk % 2, j, :], start=(kk == 0), stop=(kk == 3))
                    mm.then_inc(ada_used, 1)

            def ada_turn(c):
                pe.wait_ge(ada_out, c + 2)
                pe.wait_ge(mod_ready, c + 1)
                for b in range(4):
                    mm = pe.matmul(ada_t[:, b, :], ada_sum[:, b * P:(b + 1) * P], select, start=True, stop=True)
                mm.then_inc(ada_turned, 1)

            def sum_tokens(column, source, start, stop):
                for t, first in enumerate((0, P, T - P)):
                    mm = pe.matmul(stat[:, column + t:column + t + 1], source[:, first:first + P], ones[:, 0:1],
                                   start=start and column + t == 0, stop=stop, skip_group_check=True)
                return mm

            def spread(l, k, n):
                pe.wait_ge(norm_diag, CHAINS * l + k + 1)
                for i in range(n):
                    mm = pe.matmul(rb[i][:, 0:T], ones[:, :], diag[:, i, :], start=True, stop=True)
                mm.then_inc(norm_rb, 1)

            def sum_root(l, k, squares, n):
                pe.wait_ge(sq_added, SQUARES * l + squares + 1)
                for i in range(n):
                    mm = sum_tokens(3 * i, sq_sum[:, i, :], True, i == n - 1)
                mm.then_inc(norm_sum, 1)
                spread(l, k, n)

            def x_root(l, k, e):
                for q in range(4):
                    pe.wait_ge(x_squares, 8 * l + 4 * e + q + 1)
                    for b in range(4 * q, 4 * q + 4):
                        mm = sum_tokens(0, stage[:, b, :], b == 0, b == KD - 1)
                mm.then_inc(norm_sum, 1)
                spread(l, k, 1)

            def turn_v(l, j, slot):
                pe.wait_ge(v_normed, HA * l + j + 1)
                pe.wait_ge(v_tokens, HA * l + j + 1)
                for t, n in enumerate((P, P, T - SEQ)):
                    mm = pe.transpose(tok[0:n, t * P:(t + 1) * P], v_norm[:, slot, t * P:t * P + n], ident)
                mm.then_inc(v_turned, 1)

            def mix(l, j, slot):
                pe.wait_ge(v_tokens, HA * l + j + 2)
                pe.wait_ge(mixed_out, HA * l + j + 1)
                bias = sp_b[0:1, bass.ds(j * P, P)]
                for chunk in range(2):
                    cols = slice(chunk * P, (chunk + 1) * P)
                    pe.matmul(mixed[:, cols], v_tok[:, slot, cols], sp_w[:, bass.ds(j * P, P)],
                              start=(chunk == 0), stop=False, skip_group_check=True)
                    pe.matmul(mixed[:, cols], ones[0:1, :], bias, start=False, stop=False, skip_group_check=True)
                n = SEQS * STEP
                pe.matmul(mixed[:, SEQ:T], v_tok[0:n, slot, 2 * P:3 * P], sp_ws[0:n, bass.ds(j * n, n)],
                          start=False, stop=False, skip_group_check=True)
                pe.matmul(samples(mixed), ones[0:1, :],
                          sp_b[0:1, bass.ds(j * P, STEP)].unsqueeze(1).broadcast_to([1, SEQS, STEP]),
                          start=False, stop=True, skip_group_check=True).then_inc(mix_done, 1)

            def beside(c, unit):
                if unit == 3:
                    ada_turn(c)
                else:
                    ada_part(c, [(0,), (1,), (2, 3)][unit])

            pe.wait_ge(loaded, 16 * 5)
            pe.wait_ge(made, 4)
            pe.wait_ge(c_ready, 1)
            with pe.Fori(0, ADA_AHEAD) as c:
                ada_part(c, range(4))
                ada_turn(c)
            with pe.Fori(0, DEPTH) as l:
                c0 = ADA_AHEAD + ADA_CHUNKS * l
                x_root(l, 0, 0)
                with pe.Fori(0, HA // 4) as i:
                    for j in range(4):
                        unit_block(l, 4 * i + j, 2 * i + j // 2, j % 2, j % 2, 12 * l if j == 0 else None)
                        beside(c0 + i, j)
                sum_root(l, 1, HA, 1)
                pe.wait_ge(masked, 2 * l + 2)
                apart(pe)
                with pe.Fori(0, HB // 4) as i:
                    for jj in range(4):
                        for m in range(3):
                            n = 3 * jj + m
                            unit_block(l, HA + 12 * i + n, 6 * i + (HA + n) // 2, n % 2, n % 2)
                            beside(c0 + 2 + 3 * i + n // 4, n % 4)
                            if m == 1:
                                turn_v(l, 4 * i + jj, jj % 2)
                            if m == 2:
                                mix(l, 4 * i + jj, jj % 2)
                with pe.Fori(0, HA // 4) as i:
                    for j in range(4):
                        unit_block(l, 32 + 4 * i + j, 16 + 2 * i + j // 2, j % 2, j % 2)
                        beside(c0 + 8 + i, j)
                sum_root(l, 2, 2 * HA + HB, 2)
                with pe.Fori(0, KD // 4) as i:
                    for j in range(4):
                        unit_block(l, 40 + 4 * i + j, 20 + 2 * i + j // 2, j % 2, j % 2,
                                   12 * l + 4 if j == 0 else None)
                        beside(c0 + 10 + i, j)
                sum_root(l, 3, 2 * HA + HB + KD, 1)
                x_root(l, 4, 1)
                for n in range(8):
                    unit_block(l, A_UNITS + n, (A_BLOCKS + n) // 2, n % 2, n % 2, 12 * l + 8 if n == 0 else None)
                with pe.Fori(0, G - 1) as g:
                    u0 = A_UNITS + 8 + 12 * g
                    half = A_BLOCKS // 2 + 4 + (4 + KD // 2) * g
                    c = c0 + ADA_A + g
                    for n in range(2):
                        unit_block(l, u0 + n, half + n // 2, n % 2, n % 2)
                    with pe.If(c < ADA_TOTAL):
                        ada_part(c, (0, 1))
                    pe.wait_ge(ff_ready, 4 * G * l + 4 * g + 4)
                    for n in range(4):
                        down_unit(l, u0 + 2 + n, half + 1 + 2 * n, n % 2)
                    with pe.If(c < ADA_TOTAL):
                        ada_part(c, (2, 3))
                    for n in range(2, 8):
                        unit_block(l, u0 + 4 + n, half + (KD + n) // 2, n % 2, n % 2)
                        if n == 3:
                            with pe.If(c < ADA_TOTAL):
                                ada_turn(c)
                pe.wait_ge(ff_ready, 4 * G * l + 4 * G)
                for n in range(4):
                    down_unit(l, UNITS - 4 + n, (BLOCKS - KD) // 2 + 2 * n, n % 2)
                sum_root(l, 5, SQUARES, 1)

        @block.scalar
        def _(act):
            act.dma_start(c_raw[:, :, :], c_t).then_inc(loaded, 16)
            act.dma_start(cst[:, :], consts).then_inc(loaded, 16)
            act.dma_start(x[:, :, :], x_t).then_inc(loaded, 16)
            act.dma_start(par[:, :].rearrange("p (l n) -> p l n", l=DEPTH), params.rearrange("l p n -> p l n"))\
                .then_inc(loaded, 16)
            act.dma_start(b_ada[:, :], b_ada_t).then_inc(loaded, 16)
            act.sem_inc(ada_out, 1)
            act.sem_inc(v_tokens, 1)
            act.sem_inc(mixed_out, 1)
            act.wait_ge(loaded, 16 * 5)
            act.wait_ge(made, 4)
            act.activation(c_act[:, :, 0:R], c_raw[:, :, :], ACT.Silu).then_inc(c_ready, 1)

            def split_hi(l, u, half4):
                act.wait_ge(w_landed[half4[0]], 16 * (UNITS // RAW * l + half4[1] + 1))
                act.activation(w_hi[:, half4[0] % 2, :], w_raw[:, half4[0], :], ACT.Copy).then_inc(hi_done, 1)

            def next_hi(l, u, blocks, slot, landing):
                act.wait_ge(blocks_done, BLOCKS * l + blocks + 1)
                split_hi(l, u + 1, (slot, landing))

            def take_chunk(c):
                act.wait_ge(ada_used, 4 * c + 4)
                act.wait_ge(ada_turned, c + 1)
                act.activation(ada_sum[:, :], ada_acc[:, :], ACT.Copy).then_inc(ada_out, 1)

            def block_ready(l, b):
                act.wait_ge(blocks_done, BLOCKS * l + b + 2)

            def square_x(l, e):
                for q in range(4):
                    n = 8 * l + 4 * e + q
                    act.wait_ge(x_prompt, n + 1)
                    act.wait_ge(x_sample, n + 1)
                    act.activation(stage[:, 4 * q:4 * q + 4, :], x[:, 4 * q:4 * q + 4, :], ACT.Square)\
                        .then_inc(x_squares, 1)

            def hi_quarter(n, q):
                act.activation(h_hi[:, 4 * q:4 * q + 4, :], stage[:, 4 * q:4 * q + 4, :], ACT.Copy)\
                    .then_inc(hi_h, 1)

            def modulate_prompt(l, e):
                act.wait_ge(coef_ready, 4 * l + 2 * e + 1)
                for q in range(4):
                    n = 8 * l + 4 * e + q
                    act.wait_ge(x_scaled, n + 1)
                    for b in range(4 * q, 4 * q + 4):
                        step = act.activation(stage[:, b, 0:SEQ], stage[:, b, 0:SEQ], ACT.Identity,
                                              scale=coef_scale[:, b, 0:1], bias=coef_shift[:, b, 0:1])
                    step.then_inc(h_prompt, 1)
                    act.wait_ge(h_prompt, n + 1)
                    act.wait_ge(h_sample, 2 * n + 2)
                    hi_quarter(n, q)

            def first_tap(w, slot, out, column, bias):
                act.wait_ge(pad_hist, w + 1)
                act.activation(out, pad[:, slot, 2:PAD], ACT.Identity, scale=column(2), bias=bias)\
                    .then_inc(tap2, 1)

            with act.Fori(0, ADA_AHEAD) as c:
                take_chunk(c)
            split_hi(0, 0, (0, 0))
            with act.Fori(0, DEPTH) as l:
                c0 = ADA_AHEAD + ADA_CHUNKS * l
                square_x(l, 0)
                modulate_prompt(l, 0)
                act.activation(warm[:, 0:1], cst[:, 0:1], ACT.Gelu_apprx_tanh)
                with act.Fori(0, HA // 4) as i:
                    for j in range(4):
                        u = 4 * i + j
                        next_hi(l, u, u, (j + 1) % RAW, i + (j + 1) // 4)
                        block_ready(l, u)
                        act.activation(stage[:, u, :], main[j % 2][:, 0:T], ACT.Gelu_apprx_tanh)\
                            .then_inc(taken[j % 2], 1)
                        if j == 2:
                            take_chunk(c0 + i)
                with act.Fori(0, HB // 4) as i:
                    for jj in range(4):
                        j = 4 * i + jj
                        w = PADS * l + j
                        for m in range(3):
                            n = 3 * jj + m
                            u = HA + 12 * i + n
                            next_hi(l, u, u, (n + 1) % RAW, 2 + 3 * i + (n + 1) // 4)
                            if m == 0:
                                block_ready(l, u)
                                act.activation(gate_c[:, :], main[n % 2][:, 0:T], ACT.Copy)\
                                    .then_inc(taken[n % 2], 1)
                            if m == 1:
                                act.wait_ge(taken[n % 2], BLOCKS // 2 * l + 6 * i + (HA + n) // 2 + 2)
                                first_tap(w, jj % 2, conv_mix[:, :], lambda t: pcol(l, W_MIX + 3 * j + t), 0.0)
                                act.wait_ge(v_turned, HA * l + j + 1)
                                act.activation(v_tok[:, jj % 2, 0:SEQ], tok[:, 0:SEQ], ACT.Copy)
                                act.activation(v_tok[0:T - SEQ, jj % 2, SEQ:], tok[0:T - SEQ, SEQ:3 * P],
                                               ACT.Copy).then_inc(v_tokens, 1)
                            if m == 2:
                                act.wait_ge(mix_done, HA * l + j + 1)
                                act.activation(stage[:, j, :], mixed[:, 0:T], ACT.Copy).then_inc(mixed_out, 1)
                            if n % 4 == 2:
                                take_chunk(c0 + 2 + 3 * i + n // 4)
                with act.Fori(0, HA // 4) as i:
                    for j in range(4):
                        u = 32 + 4 * i + j
                        next_hi(l, u, u, (j + 1) % RAW, 8 + i + (j + 1) // 4)
                        block_ready(l, u)
                        act.wait_ge(a_ready, HA * l + 4 * i + j + 1)
                        act.activation(u_act[:, :], main[j % 2][:, 0:T], ACT.Gelu_apprx_tanh)\
                            .then_inc(taken[j % 2], 1)
                        if j == 2:
                            take_chunk(c0 + 8 + i)
                for q in range(4):
                    act.wait_ge(ab_scaled, 4 * l + q + 1)
                    hi_quarter(12 * l + 4 + q, q)
                with act.Fori(0, KD // 4) as i:
                    for j in range(4):
                        u = 40 + 4 * i + j
                        next_hi(l, u, u, (j + 1) % RAW, 10 + i + (j + 1) // 4)
                        block_ready(l, u)
                        act.activation(stage[:, 4 * i + j, :], main[j % 2][:, 0:T], ACT.Copy)\
                            .then_inc(taken[j % 2], 1)
                        if j == 2:
                            take_chunk(c0 + 10 + i)
                square_x(l, 1)
                modulate_prompt(l, 1)

                def take_row(l, g, n, b, half):
                    w = PADS * l + HB + 8 * g + n
                    block_ready(l, b)
                    act.wait_ge(conv_done, w + 1)
                    act.wait_ge(pad_kept, w + 1)
                    act.activation(pad[:, n % 2, 2:S0], main[n % 2][:, 0:SEQ], ACT.Copy)
                    act.activation(padded(pad[:, n % 2, :], 2, STEP), samples(main[n % 2]), ACT.Copy)\
                        .then_inc(taken[n % 2], 1)
                    act.wait_ge(taken[n % 2], BLOCKS // 2 * l + half + 2)
                    column = W_CF + 4 * (8 * g + n)
                    first_tap(w, n % 2, conv_ffn[:, n % 2, :], lambda t: pcol(l, column + t), pcol(l, column + 3))

                def gate(l, g, pair):
                    act.wait_ge(conv_done, PADS * l + HB + 8 * g + 2 * pair + 3)
                    act.activation(gate_act[:, :], conv_ffn[:, 0, :], ACT.Silu).then_inc(gate_done, 1)

                def ff_hi_part(l, g, pair):
                    act.wait_ge(ff_done, 4 * (G * l + g) + pair + 1)
                    act.activation(ff_hi[:, pair, :], ff[:, :], ACT.Copy).then_inc(ff_hi_done, 1)

                act.activation(warm[:, 1:2], cst[:, 0:1], ACT.Silu)
                for n in range(8):
                    u = A_UNITS + n
                    next_hi(l, u, A_BLOCKS + n, (n + 1) % RAW, (u + 1) // RAW)
                    if n % 2 == 0 and n:
                        ff_hi_part(l, 0, n // 2 - 1)
                    take_row(l, 0, n, A_BLOCKS + n, (A_BLOCKS + n) // 2)
                    if n % 2:
                        gate(l, 0, n // 2)
                with act.Fori(0, G - 1) as g:
                    u0 = A_UNITS + 8 + 12 * g
                    b0 = A_BLOCKS + 8 + (8 + KD) * g
                    half = A_BLOCKS // 2 + 4 + (4 + KD // 2) * g
                    landing = (A_UNITS + 8) // RAW + 3 * g
                    c = c0 + ADA_A + g
                    for n in range(12):
                        if n < 2:
                            block, row = n, n
                        elif n < 6:
                            block, row = 2 + 4 * (n - 2), None
                        else:
                            block, row = n - 4 + KD, n - 4
                        next_hi(l, u0 + n, b0 + block, (n + 1) % RAW, landing + (n + 1) // 4)
                        if n == 0:
                            ff_hi_part(l, g, 3)
                        elif row is not None and row % 2 == 0:
                            ff_hi_part(l, g + 1, row // 2 - 1)
                        if row is not None:
                            take_row(l, g + 1, row, b0 + block, half + block // 2)
                            if row % 2:
                                gate(l, g + 1, row // 2)
                        if n == 6:
                            with act.If(c < ADA_TOTAL):
                                take_chunk(c)
                ff_hi_part(l, G - 1, 3)
                for n in range(3):
                    next_hi(l, UNITS - 4 + n, BLOCKS - KD + 4 * n, n + 1, UNITS // RAW - 1)
                with act.If(l < DEPTH - 1):
                    next_hi(l, UNITS - 1, BLOCKS - 4, 0, UNITS // RAW)

        @block.vector
        def _(dve):
            dve.sem_inc(split_done, RAW)
            for s in taken:
                dve.sem_inc(s, 1)
            dve.sem_inc(mod_ready, 1)
            dve.sem_inc(a_ready, 1)
            dve.sem_inc(conv_done, 2)
            dve.sem_inc(x_prompt, 4)
            dve.wait_ge(loaded, 16 * 5)

            def split_lo(u, slot):
                dve.wait_ge(hi_done, u + 1)
                dve.tensor_tensor(w_lo[:, slot % 2, :], w_raw[:, slot, :], w_hi[:, slot % 2, :].bitcast(F32),
                                  ALU.subtract).then_inc(split_done, 1)

            def take_mod(c):
                dve.wait_ge(ada_turned, c + 2)
                dve.tensor_tensor(mod[:, bass.ds(4 * c, 4), :], ada_t,
                                  b_ada[:, bass.ds(4 * c, 4)].unsqueeze(2).broadcast_to([P, 4, R]), ALU.add)\
                    .then_inc(mod_ready, 1)

            def mod_of(l, which):
                return mod[:, bass.ds(6 * KD * l + KD * which, KD), :]

            def gains(l, column):
                return par[:, bass.ds(l * NPAR + column, KD)].unsqueeze(2).broadcast_to([P, KD, R])

            def modulation(l, scale, shift, gain, chunks):
                dve.wait_ge(mod_ready, ADA_CHUNKS * l + chunks + 1)
                dve.tensor_copy(coef_shift[:, :, :], mod_of(l, shift))
                dve.scalar_tensor_tensor(coef_scale[:, :, :], mod_of(l, scale), 1.0, gains(l, gain), ALU.add,
                                         ALU.mult).then_inc(coef_ready, 1)

            def gating(l, gate, gain, chunks):
                dve.wait_ge(mod_ready, ADA_CHUNKS * l + chunks + 1)
                dve.tensor_tensor(coef_gate[:, :, :], mod_of(l, gate), gains(l, gain), ALU.mult)\
                    .then_inc(coef_ready, 1)

            def root(l, k, n, width):
                dve.wait_ge(norm_sum, CHAINS * l + k + 1)
                dve.tensor_scalar(var[:, 0:3 * n], stat[:, 0:3 * n], 1.0 / width, EPS, ALU.mult, ALU.add)\
                    .then_inc(norm_var, 1)
                dve.wait_ge(norm_rstd, CHAINS * l + k + 1)
                for i in range(n):
                    dve.tensor_scalar(diag[:, i, 0:P], ident, rstd[:, 3 * i:3 * i + 1], None, ALU.mult)
                    dve.tensor_scalar(diag[:, i, P:2 * P], ident, rstd[:, 3 * i + 1:3 * i + 2], None, ALU.mult)
                    step = dve.tensor_scalar(diag[:, i, SEQ:T], ident[:, P - (T - SEQ):P],
                                             rstd[:, 3 * i + 2:3 * i + 3], None, ALU.mult)
                step.then_inc(norm_diag, 1)
                dve.wait_ge(norm_rb, CHAINS * l + k + 1)
                apart(dve)

            def lo_quarter(n, q):
                dve.wait_ge(hi_h, n + 1)
                quarter = slice(4 * q, 4 * q + 4)
                dve.tensor_tensor(h_lo[:, quarter, :], stage[:, quarter, :], h_hi[:, quarter, :].bitcast(F32),
                                  ALU.subtract).then_inc(h_ready, 1)

            def normed_h(l, e, n):
                for q in range(5):
                    if q < 4:
                        quarter = slice(4 * q, 4 * q + 4)
                        dve.tensor_tensor(stage[:, quarter, :], x[:, quarter, :], over_blocks(rb[0], 4), ALU.mult)\
                            .then_inc(x_scaled, 1)
                    if q:
                        lo_quarter(12 * l + n + q - 1, q - 1)

            def update_x(l, e):
                for q in range(4):
                    quarter = slice(4 * q, 4 * q + 4)
                    n = 8 * l + 4 * e + q
                    dve.tensor_tensor(stage[:, quarter, :], stage[:, quarter, :], over_blocks(rb[0], 4), ALU.mult)\
                        .then_inc(post_scaled, 1)
                    dve.wait_ge(post_scaled, n + 1)
                    for b in range(4 * q, 4 * q + 4):
                        step = dve.scalar_tensor_tensor(x[:, b, 0:SEQ], stage[:, b, 0:SEQ], coef_gate[:, b, 0:1],
                                                        x[:, b, 0:SEQ], ALU.mult, ALU.add)
                    step.then_inc(x_prompt, 1)

            def other_taps(w, slot, row, column):
                dve.wait_ge(tap2, w + 1)
                dve.scalar_tensor_tensor(row, pad[:, slot, 1:PAD - 1], column(1), row, ALU.mult, ALU.add)\
                    .then_inc(tap1, 1)
                dve.wait_ge(tap1, w + 1)
                dve.scalar_tensor_tensor(row, pad[:, slot, 0:PAD - 2], column(0), row, ALU.mult, ALU.add)\
                    .then_inc(conv_done, 1)

            def block_ready(l, b):
                dve.wait_ge(blocks_done, BLOCKS * l + b + 2)

            with dve.Fori(0, ADA_AHEAD) as c:
                take_mod(c)
            split_lo(0, 0)
            with dve.Fori(0, DEPTH) as l:
                u0 = UNITS * l
                c0 = ADA_AHEAD + ADA_CHUNKS * l
                modulation(l, SCALE1, SHIFT1, G_PRE_MIX, 8)
                root(l, 0, 1, D_MODEL)
                normed_h(l, 0, 0)
                with dve.Fori(0, HA // 4) as i:
                    for j in range(4):
                        split_lo(u0 + 4 * i + j + 1, (j + 1) % RAW)
                    take_mod(c0 + i)
                root(l, 1, 1, W_A)
                with dve.Fori(0, HB // 4) as i:
                    for jj in range(4):
                        j = 4 * i + jj
                        w = PADS * l + j
                        for m in range(3):
                            n = 3 * jj + m
                            u = HA + 12 * i + n
                            split_lo(u0 + u + 1, (n + 1) % RAW)
                            bank = main[n % 2]
                            half = BLOCKS // 2 * l + 6 * i + (HA + n) // 2 + 2
                            if m == 0:
                                dve.wait_ge(v_free, HA * l + j + 1)
                                dve.wait_ge(v_tokens, HA * l + j + 1)
                                dve.scalar_tensor_tensor(v_norm[:, jj % 2, :], stage[:, j, :], pcol(l, G_V + j),
                                                         rb[0][:, 0:T], ALU.mult, ALU.mult).then_inc(v_normed, 1)
                            if m == 1:
                                block_ready(l, u)
                                dve.wait_ge(taken[(n - 1) % 2], BLOCKS // 2 * l + 6 * i + (HA + n - 1) // 2 + 2)
                                dve.wait_ge(pad_kept, w + 1)
                                row = pad[:, jj % 2, :]
                                dve.tensor_tensor(row[:, 2:S0], gate_c[:, 0:SEQ], bank[:, 0:SEQ], ALU.mult)
                                dve.tensor_tensor(padded(row, 2, STEP), samples(gate_c), samples(bank), ALU.mult)\
                                    .then_inc(taken[n % 2], 1)
                                other_taps(w, jj % 2, conv_mix[:, :], lambda t: pcol(l, W_MIX + 3 * j + t))
                            if m == 2:
                                block_ready(l, u)
                                dve.wait_ge(conv_done, w + 3)
                                dve.tensor_tensor(stage[:, HA + j, 0:SEQ], conv_mix[:, 0:SEQ], bank[:, 0:SEQ],
                                                  ALU.mult)
                                dve.tensor_tensor(samples(stage[:, HA + j, :]), conv_samples(conv_mix),
                                                  samples(bank), ALU.mult).then_inc(taken[n % 2], 1)
                            if n % 4 == 3:
                                take_mod(c0 + 2 + 3 * i + n // 4)
                with dve.Fori(0, HA // 4) as i:
                    for j in range(4):
                        split_lo(u0 + 32 + 4 * i + j + 1, (j + 1) % RAW)
                        dve.wait_ge(taken[j % 2], BLOCKS // 2 * l + 16 + 2 * i + j // 2 + 2)
                        dve.wait_ge(mixed_out, HA * l + 4 * i + j + 2)
                        dve.tensor_tensor(stage[:, 4 * i + j, :], stage[:, 4 * i + j, :], u_act[:, :], ALU.mult)\
                            .then_inc(a_ready, 1)
                    take_mod(c0 + 8 + i)
                root(l, 2, 2, W_A)
                for q in range(5):
                    if q < 4:
                        for b in range(4 * q, 4 * q + 4):
                            step = dve.scalar_tensor_tensor(stage[:, b, :], stage[:, b, :], pcol(l, G_OUT + b),
                                                            rb[b // HA][:, 0:T], ALU.mult, ALU.mult)
                        step.then_inc(ab_scaled, 1)
                    if q:
                        lo_quarter(12 * l + 4 + q - 1, q - 1)
                with dve.Fori(0, KD // 4) as i:
                    for j in range(4):
                        split_lo(u0 + 40 + 4 * i + j + 1, (j + 1) % RAW)
                    take_mod(c0 + 10 + i)
                gating(l, GATE1, G_POST_MIX, 12)
                root(l, 3, 1, D_MODEL)
                update_x(l, 0)
                modulation(l, SCALE2, SHIFT2, G_PRE_FFN, 20)
                root(l, 4, 1, D_MODEL)
                normed_h(l, 1, 8)

                def conv_row(l, g, n):
                    column = W_CF + 4 * (8 * g + n)
                    other_taps(PADS * l + HB + 8 * g + n, n % 2, conv_ffn[:, n % 2, :],
                               lambda t: pcol(l, column + t))

                def multiply(l, g, pair):
                    dve.wait_ge(gate_done, 4 * (G * l + g) + pair + 1)
                    dve.wait_ge(conv_done, PADS * l + HB + 8 * g + 2 * pair + 4)
                    dve.tensor_tensor(ff[:, 0:SEQ], gate_act[:, 0:SEQ], conv_ffn[:, 1, 0:SEQ], ALU.mult)
                    dve.tensor_tensor(samples(ff), conv_samples(gate_act), conv_samples(conv_ffn[:, 1, :]),
                                      ALU.mult).then_inc(ff_done, 1)

                def ff_lo_part(l, g, pair):
                    dve.wait_ge(ff_hi_done, 4 * (G * l + g) + pair + 1)
                    dve.tensor_tensor(ff_lo[:, pair, :], ff[:, :], ff_hi[:, pair, :].bitcast(F32), ALU.subtract)\
                        .then_inc(ff_ready, 1)

                def add_down(l, b0, n, first=0, end=4):
                    for m in range(first, end):
                        block_ready(l, b0 + m)
                        dve.tensor_tensor(stage[:, 4 * n + m, :], stage[:, 4 * n + m, :], main[m % 2][:, 0:T],
                                          ALU.add).then_inc(taken[m % 2], 1)

                for n in range(8):
                    split_lo(u0 + A_UNITS + n + 1, (n + 1) % RAW)
                    if n % 2 == 0 and n:
                        ff_lo_part(l, 0, n // 2 - 1)
                    conv_row(l, 0, n)
                    if n % 2:
                        multiply(l, 0, n // 2)
                dve.wait_ge(zeroed, l + 1)
                apart(dve)
                with dve.Fori(0, G - 1) as g:
                    b0 = A_BLOCKS + 8 + (8 + KD) * g
                    c = c0 + ADA_A + g
                    for n in range(12):
                        unit = u0 + A_UNITS + 8 + 12 * g + n + 1
                        if 2 <= n < 6:
                            add_down(l, b0 + 2 + 4 * (n - 2), n - 2, 0, 1)
                            split_lo(unit, (n + 1) % RAW)
                            add_down(l, b0 + 2 + 4 * (n - 2), n - 2, 1, 4)
                            continue
                        split_lo(unit, (n + 1) % RAW)
                        row = n if n < 2 else n - 4
                        if row == 0:
                            ff_lo_part(l, g, 3)
                        elif row % 2 == 0:
                            ff_lo_part(l, g + 1, row // 2 - 1)
                        conv_row(l, g + 1, row)
                        if row % 2:
                            multiply(l, g + 1, row // 2)
                        if n == 8:
                            with dve.If(c < ADA_TOTAL):
                                take_mod(within(c, ADA_TOTAL))
                ff_lo_part(l, G - 1, 3)
                for n in range(3):
                    add_down(l, BLOCKS - KD + 4 * n, n, 0, 1)
                    split_lo(u0 + UNITS - 4 + n + 1, n + 1)
                    add_down(l, BLOCKS - KD + 4 * n, n, 1, 4)
                with dve.If(l < DEPTH - 1):
                    split_lo(u0 + UNITS, 0)
                add_down(l, BLOCKS - 4, 3)
                gating(l, GATE2, G_POST_FFN, 24)
                root(l, 5, 1, D_MODEL)
                update_x(l, 1)


_OUTS = [
    ("y_t", (P, KD, T)),
    ("new_mix", (DEPTH, P, HB * R * 2)),
    ("new_ffn", (DEPTH, G, P, 8 * R * 2)),
    ("v_rows", (DEPTH, HA, P, T - P)),
]


def kernel(x_prompt, x_sample, state_conv_mix, state_conv_ffn, c_prompt, c_sample,
           w_ada, b_ada, g_pre_mix, g_post_mix, g_pre_ffn, g_post_ffn,
           w_in, g_v, w_spatial, b_spatial, w_conv_mix, g_out_a, g_out_b, w_out,
           w_up, w_conv_ffn, b_conv_ffn, w_down):
    import numpy as np
    import concourse.bacc as bacc
    from concourse.bass_utils import run_bass_kernel_spmd

    f = np.float32

    def by_partition(a):
        a = np.asarray(a)
        return a.reshape(a.shape[0], -1, P).transpose(0, 2, 1)

    tokens = np.concatenate([np.asarray(x_prompt).reshape(SEQ, D_MODEL),
                             np.asarray(x_sample).reshape(SEQS * STEP, D_MODEL)])
    x_t = tokens.reshape(T, KD, P).transpose(2, 1, 0)
    rows = np.concatenate([np.asarray(c_prompt), np.asarray(c_sample)])
    c_t = rows.reshape(R, KD, P).transpose(2, 1, 0)
    select = (np.arange(P)[:, None] % 32 == np.arange(R)[None, :]).astype(f)
    consts = np.concatenate([np.eye(P, dtype=f), select], axis=1)

    def by_pair(a, axis):
        a = np.moveaxis(np.asarray(a), axis, -1)
        a = a.reshape(a.shape[:-1] + (2, 4 * G, P))
        return np.moveaxis(a, -3, -2)

    taps = by_pair(w_conv_ffn, 2).reshape(DEPTH, 3, 8 * G, P)
    bias = by_pair(b_conv_ffn, 1).reshape(DEPTH, 1, 8 * G, P)
    conv_ffn = np.concatenate([taps, bias], axis=1).transpose(0, 3, 2, 1).reshape(DEPTH, P, -1)
    conv_mix = np.asarray(w_conv_mix).reshape(DEPTH, 3, HB, P).transpose(0, 3, 2, 1).reshape(DEPTH, P, -1)
    params = np.concatenate(
        [by_partition(a) for a in (g_pre_mix, g_post_mix, g_pre_ffn, g_post_ffn, g_v, g_out_a, g_out_b)]
        + [conv_mix, conv_ffn], axis=2)
    assert params.shape[2] == NPAR
    b_ada_t = np.asarray(b_ada).reshape(DEPTH * 6 * KD, P).T

    mix_hist = np.asarray(state_conv_mix).reshape(SEQS, DEPTH, 2, HB, P).transpose(1, 4, 3, 0, 2)
    ffn_hist = by_pair(state_conv_ffn, 3).reshape(SEQS, DEPTH, 2, G, 8, P).transpose(1, 3, 5, 4, 0, 2)

    ws = np.asarray(w_spatial)
    w_sp = ws.transpose(0, 3, 1, 2)
    w_sp_s = np.zeros((DEPTH, SEQS * STEP, HA, SEQS, STEP), f)
    for s in range(SEQS):
        w_sp_s[:, s * STEP:(s + 1) * STEP, :, s, :] = ws[:, :, :STEP, :STEP].transpose(0, 3, 1, 2)
    b_sp = np.asarray(b_spatial).reshape(DEPTH, 1, HA * P)

    ada_units = np.asarray(w_ada).reshape(DEPTH, 4, 4, P, ADA_CHUNKS, 512).transpose(0, 4, 1, 3, 2, 5)
    ada_units = np.ascontiguousarray(ada_units).reshape(ADA_TOTAL * 4, P, 4, 512)

    w_units = np.empty((DEPTH * UNITS, P, UNIT), f)
    w_in, w_out, w_up, w_down = (np.asarray(a) for a in (w_in, w_out, w_up, w_down))
    n = 0

    def put(a):
        nonlocal n
        tiles = a.shape[0] // P
        w_units[n] = a.reshape(tiles, P, a.shape[1]).transpose(1, 0, 2).reshape(P, UNIT)
        n += 1

    for l in range(DEPTH):
        def columns(w, first):
            put(w[l, :, first:first + P])

        def down(g):
            for q in range(4):
                put(w_down[l, 512 * g:512 * (g + 1), 512 * q:512 * (q + 1)])

        for j in range(HA):
            columns(w_in, W_A + j * P)
        for j in range(HB):
            for part in (1, 2, 0):
                columns(w_in, 2 * W_A + part * W_B + j * P)
        for j in range(HA):
            columns(w_in, j * P)
        for m in range(KD):
            columns(w_out, m * P)
        for g in range(G):
            for j in range(4):
                for part in range(2):
                    columns(w_up, part * D_FF + (4 * g + j) * P)
                if j == 0 and g:
                    down(g - 1)
        down(G - 1)
    assert n == DEPTH * UNITS

    arrays = {
        "x_t": x_t, "c_t": c_t, "consts": consts, "params": params, "b_ada_t": b_ada_t,
        "mix_hist": mix_hist.reshape(DEPTH, P, -1), "ffn_hist": ffn_hist.reshape(DEPTH, G, P, -1),
        "w_sp": w_sp.reshape(DEPTH, P, -1), "w_sp_s": w_sp_s.reshape(DEPTH, SEQS * STEP, -1), "b_sp": b_sp,
        "ada_units": ada_units, "w_units": w_units,
    }
    arrays = {k: np.ascontiguousarray(v) for k, v in arrays.items()}
    nc = bacc.Bacc("TRN2", target_bir_lowering=False, num_devices=1)
    args = [nc.dram_tensor(k, v.shape, F32, kind="ExternalInput").ap() for k, v in arrays.items()]
    args += [nc.dram_tensor(k, shape, F32, kind="ExternalOutput").ap() for k, shape in _OUTS]
    trunk_kernel(nc, *args)
    r = run_bass_kernel_spmd(nc, [arrays], core_ids=[0]).results[0]

    y = r["y_t"].transpose(2, 1, 0).reshape(T, D_MODEL)
    mix = r["new_mix"].reshape(DEPTH, P, HB, R, 2).transpose(3, 0, 4, 2, 1).reshape(R, DEPTH, 2, W_B)
    ffn = r["new_ffn"].reshape(DEPTH, G, P, 4, 2, R, 2).transpose(5, 0, 6, 4, 1, 3, 2)
    ffn = ffn.reshape(R, DEPTH, 2, 2 * D_FF)
    v = r["v_rows"].transpose(0, 3, 1, 2).reshape(DEPTH, T - P, W_A)
    v_prompt = v[None, :, 0:P]
    v_sample = v[:, P:].reshape(DEPTH, SEQS, STEP, W_A).transpose(1, 0, 2, 3)
    return (y[:SEQ].reshape(1, SEQ, D_MODEL), y[SEQ:].reshape(SEQS, STEP, D_MODEL),
            mix[:1], mix[1:], ffn[:1], ffn[1:], v_prompt, v_sample)
```

```python
from contextlib import ExitStack

import concourse.bass as bass
from concourse import mybir

F32 = mybir.dt.float32
F32R = mybir.dt.float32r
ALU = mybir.AluOpType
ACT = mybir.ActivationFunctionType

P = 128
DEPTH = 2
D_MODEL = 2048
SEQ = 256
SEQS = 8
STEP = 8
W_A = 1024
W_B = 1024
D_FF = 5632
EPS = 1e-6

T = SEQ + SEQS * STEP
R = 1 + SEQS
KD = D_MODEL // P
HA = W_A // P
HB = W_B // P
PAD = 2 + SEQ + SEQS * (2 + STEP)
CONV = PAD - 2
SROW = 2 + STEP
S0 = 2 + SEQ
G = D_FF // (4 * P)

UNIT = 2048
RAW = 4
SPLIT = 2
U_UNIT = HA + 3 * HB
OUT_UNIT = U_UNIT + HA
A_UNITS = OUT_UNIT + KD
UNITS = A_UNITS + G * 12
A_BLOCKS = A_UNITS
BLOCKS = A_BLOCKS + G * (8 + KD)
ADA_CHUNKS = 6 * D_MODEL // 512
ADA_TOTAL = DEPTH * ADA_CHUNKS
ADA_AHEAD = 8
ADA_A = A_UNITS // 4
ADA_MID = 2
ADA_FFN = ADA_CHUNKS - ADA_A - ADA_MID
ADA_END = 1
ADA_STEP = ADA_A + ADA_MID + ADA_FFN + ADA_END
assert ADA_AHEAD + (DEPTH - 1) * ADA_STEP + ADA_A + 1 == ADA_TOTAL
SHIFT1, SCALE1, GATE1, SHIFT2, SCALE2, GATE2 = range(6)

G_PRE_MIX, G_POST_MIX, G_PRE_FFN, G_POST_FFN = 0, KD, 2 * KD, 3 * KD
G_V = 4 * KD
G_OUT = G_V + HA
W_MIX = G_OUT + KD
W_CF = W_MIX + 3 * HB
NPAR = W_CF + 4 * 8 * G

OUT_ORDER = (2, 3, 0, 1)
UPDATE_ORDER = (0, 1, 3, 2)

CHAINS = 7
SQUARES = HA + HB + HA + KD + KD
PADS = HB + 8 * G


def trunk_kernel(nc, x_t, c_t, consts, params, b_ada_t, mix_hist, ffn_hist, w_sp, w_sp_s, b_sp, ada_units,
                 w_units, y_t, new_mix, new_ffn, v_rows):
    with ExitStack() as ctx:
        at = [(nc.sbuf_base + 63) // 64 * 64]

        def place(name, shape, dtype=F32, offset=None):
            size = 4
            for n in shape[1:]:
                size *= n
            here = at[0] if offset is None else offset
            tensor = nc.alloc_sbuf_tensor_at(name, shape, dtype, offset=here)
            if offset is None:
                at[0] += (size + 31) // 32 * 32
            return tensor, here + (size + 31) // 32 * 32

        def sb(name, shape, dtype=F32):
            return place(name, shape, dtype)[0]

        def sem(name):
            return ctx.enter_context(nc.semaphore(name))

        x = sb("x", [P, KD, T])
        h_hi = sb("h_hi", [P, KD, T], F32R)
        h_lo = sb("h_lo", [P, KD, T], F32R)
        w_raw = sb("w_raw", [P, RAW, UNIT])
        w_hi = sb("w_hi", [P, SPLIT, UNIT], F32R)
        w_lo = sb("w_lo", [P, SPLIT, UNIT], F32R)
        ada_raw = sb("ada_raw", [P, 2, 4, 512])
        stage = sb("stage", [P, KD, T])
        mod = sb("mod", [P, DEPTH * 6 * KD, R])
        pad = sb("pad", [P, 2, PAD])
        ada_sum = sb("ada_sum", [P, 512])
        sq_sum = sb("sq_sum", [P, 2, T])
        sq = sb("sq", [P, T])
        diag = sb("diag", [P, 2, T])
        par = sb("par", [P, DEPTH * NPAR])
        b_ada = sb("b_ada", [P, DEPTH * 6 * KD])
        coef_scale = sb("coef_scale", [P, KD, R])
        coef_shift = sb("coef_shift", [P, KD, R])
        coef_gate = sb("coef_gate", [P, KD, R])
        c_act = sb("c_act", [P, KD, 32])
        cst = sb("cst", [P, P + R])
        ones = sb("ones", [P, P])
        mix_new = sb("mix_new", [P, HB, R, 2])
        mix_old = sb("mix_old", [P, HB, SEQS, 2])
        var = sb("var", [P, 3])
        rstd = sb("rstd", [P, 3])
        minus_half = sb("minus_half", [P, 3])
        warm = sb("warm", [P, 2])
        ident = cst[:, 0:P]
        select = cst[:, P:P + R]

        zone = at[0]
        c_raw, _ = place("c_raw", [P, KD, R], F32, zone)
        v_norm, e = place("v_norm", [P, 2, T], F32, zone)
        v_tok, e = place("v_tok", [P, 2, 3 * P], F32, e)
        sp_w, e = place("sp_w", [P, HA * P], F32, e)
        sp_ws, e = place("sp_ws", [SEQS * STEP, HA * SEQS * STEP], F32, e)
        sp_b, e = place("sp_b", [1, HA * P], F32, e)
        gate_c, e = place("gate_c", [P, T], F32, e)
        conv_mix, e = place("conv_mix", [P, CONV], F32, e)
        u_act, end_mix = place("u_act", [P, T], F32, e)
        ff_hi, e = place("ff_hi", [P, 4, T], F32R, zone)
        ff_lo, e = place("ff_lo", [P, 4, T], F32R, e)
        ffn_old, e = place("ffn_old", [P, 8, SEQS, 2], F32, e)
        ffn_new, e = place("ffn_new", [P, 8, R, 2], F32, e)
        conv_ffn, e = place("conv_ffn", [P, 2, CONV], F32, e)
        gate_act, e = place("gate_act", [P, CONV], F32, e)
        ff, end_ffn = place("ff", [P, T], F32, e)
        assert max(end_mix, end_ffn) <= nc.sbuf_usable_end, (end_mix, end_ffn, nc.sbuf_usable_end)

        main = [ctx.enter_context(nc.psum_tensor(f"main{i}", [P, 512], F32)) for i in range(2)]
        ada_acc = ctx.enter_context(nc.psum_tensor("ada_acc", [P, 512], F32))
        ada_turn_acc = ctx.enter_context(nc.psum_tensor("ada_turn_acc", [P, 512], F32))
        rb = [ctx.enter_context(nc.psum_tensor(f"rb{i}", [P, 512], F32)) for i in range(2)]
        tok = ctx.enter_context(nc.psum_tensor("tok", [P, 512], F32))
        mixed = ctx.enter_context(nc.psum_tensor("mixed", [P, 512], F32))
        ada_t = ada_turn_acc[:, 0:4 * R].rearrange("p (b r) -> p b r", r=R)
        stat = tok[:, 3 * P:3 * P + 3]

        c_loaded = sem("c_loaded")
        loaded = sem("loaded")
        w_landed = [sem(f"w_landed{i}") for i in range(RAW)]
        ada_landed = [sem(f"ada_landed{i}") for i in range(2)]
        ahead_landed = [sem(f"ahead_landed{i}") for i in range(4)]
        mix_landed = sem("mix_landed")
        hist_landed = sem("hist_landed")
        v_saved = [sem(f"v_saved{i}") for i in range(2)]
        mix_saved = sem("mix_saved")
        ffn_saved = sem("ffn_saved")
        y_saved = sem("y_saved")
        made = sem("made")
        c_ready = sem("c_ready")
        hi_done = sem("hi_done")
        split_done = sem("split_done")
        blocks_done = sem("blocks_done")
        taken = [sem(f"taken{i}") for i in range(2)]
        ada_used = sem("ada_used")
        ada_out = sem("ada_out")
        ada_turned = sem("ada_turned")
        mod_ready = sem("mod_ready")
        coef_ready = sem("coef_ready")
        sq_reset = sem("sq_reset")
        sq_one = sem("sq_one")
        sq_added = sem("sq_added")
        norm_sum = sem("norm_sum")
        norm_var = sem("norm_var")
        norm_rstd = sem("norm_rstd")
        norm_diag = sem("norm_diag")
        norm_rb = sem("norm_rb")
        norm_rb_last = sem("norm_rb_last")
        rows_last = sem("rows_last")
        gated_prompt = sem("gated_prompt")
        gated_sample = sem("gated_sample")
        scaled_first = sem("scaled_first")
        scaled_last = sem("scaled_last")
        x_first = sem("x_first")
        x_last = sem("x_last")
        x_squares = sem("x_squares")
        x_summed = sem("x_summed")
        x_copied = sem("x_copied")
        x_scaled = sem("x_scaled")
        h_prompt = sem("h_prompt")
        h_sample = sem("h_sample")
        ab_scaled = sem("ab_scaled")
        hi_h = sem("hi_h")
        h_ready = sem("h_ready")
        masked = sem("masked")
        v_normed = sem("v_normed")
        v_free = sem("v_free")
        v_turned = sem("v_turned")
        v_tokens = sem("v_tokens")
        mix_done = sem("mix_done")
        mixed_out = sem("mixed_out")
        a_ready = sem("a_ready")
        pad_hist = sem("pad_hist")
        pad_kept = sem("pad_kept")
        tap2 = sem("tap2")
        tap1 = sem("tap1")
        conv_done = sem("conv_done")
        gate_done = sem("gate_done")
        ff_done = sem("ff_done")
        ff_hi_done = sem("ff_hi_done")
        ff_ready = sem("ff_ready")
        zeroed = sem("zeroed")
        passed = sem("passed")

        def within(index, n):
            return nc.s_assert_within(index, 0, n - 1, skip_runtime_bounds_check_because="an If checks it")

        def pcol(l, column):
            return par[:, bass.ds(l * NPAR + column, 1)]

        def samples(row):
            return row[:, SEQ:T].rearrange("p (s t) -> p s t", t=STEP)

        def padded(row, first, n):
            return row[:, S0:PAD].rearrange("p (s t) -> p s t", t=SROW)[:, :, first:first + n]

        def conv_samples(row):
            return row[:, SEQ:CONV].rearrange("p (s t) -> p s t", t=SROW)[:, :, 2:SROW]

        def quarter_samples(t, q):
            return t[:, 4 * q:4 * q + 4, SEQ:T].rearrange("p b (s t) -> p b s t", t=STEP)

        def per_sample(coef, q):
            return coef[:, 4 * q:4 * q + 4, 1:R].unsqueeze(3).broadcast_to([P, 4, SEQS, STEP])

        def ahead_buffer(kk):
            if kk < 2:
                return ada_raw[:, kk, :, :]
            return w_raw[:, kk, :].rearrange("p (j n) -> p j n", n=512)

        def ffn_chunk(l, g):
            return ADA_AHEAD + ADA_STEP * l + ADA_A + ADA_MID + g

        def over_blocks(bank, n):
            return bank[:, 0:T].unsqueeze(1).broadcast_to([P, n, T])

        def apart(eng):
            eng.sem_inc(passed, 1)

        block = ctx.enter_context(nc.Block())

        @block.sync
        def _(sp):
            def load_w(u, slot):
                sp.wait_ge(split_done, u + 1)
                sp.dma_start(w_raw[:, slot, :], w_units[u]).then_inc(w_landed[slot], 16)

            def load_ada(a, slot):
                sp.wait_ge(ada_used, a - 1)
                sp.dma_start(ada_raw[:, slot, :, :], ada_units[a]).then_inc(ada_landed[slot], 16)

            ahead = [ahead_buffer(kk) for kk in range(4)]
            for kk in range(4):
                sp.dma_start(ahead[kk], ada_units[kk]).then_inc(ahead_landed[kk], 16)
            for u in range(2):
                load_w(u, u)
            with sp.Fori(1, ADA_AHEAD) as c:
                for kk in range(4):
                    sp.wait_ge(ada_used, 4 * c + kk - 3)
                    sp.dma_start(ahead[kk], ada_units[4 * c + kk]).then_inc(ahead_landed[kk], 16)
            sp.wait_ge(ada_used, 4 * ADA_AHEAD)
            with sp.Fori(0, DEPTH) as l:
                w0 = UNITS * l
                a0 = 4 * (ADA_AHEAD + ADA_STEP * l)
                with sp.Fori(0, ADA_A - 1) as i:
                    for j in range(4):
                        load_w(w0 + 4 * i + 2 + j, (2 + j) % RAW)
                        load_ada(a0 + 4 * i + j, j % 2)
                for j in range(4):
                    load_w(w0 + A_UNITS - 2 + j, (2 + j) % RAW)
                    if j != 1:
                        load_ada(a0 + 4 * ADA_A - 4 + j - (j > 1), (j - (j > 1)) % 2)
                load_ada(a0 + 4 * ADA_A - 1, 1)
                for u in range(2, 8):
                    load_w(w0 + A_UNITS + u, u % RAW)
                    if u == 3:
                        for j in range(2):
                            load_ada(a0 + 4 * ADA_A + j, j)
                    if u == 4:
                        for j in range(2, 4):
                            load_ada(a0 + 4 * ADA_A + j, j % 2)
                        with sp.If(l < DEPTH - 1):
                            for j in range(4):
                                load_ada(within(a0 + 4 * ADA_A + 4 + j, 4 * ADA_TOTAL), j % 2)
                with sp.Fori(0, G - 1) as g:
                    for part in range(3):
                        for j in range(4):
                            load_w(w0 + A_UNITS + 8 + 12 * g + 4 * part + j, j)
                        if part < 2:
                            with sp.If(ffn_chunk(l, g) < ADA_CHUNKS + ADA_AHEAD):
                                for j in range(2):
                                    a = within(4 * ffn_chunk(l, g) + 2 * part + j, 4 * ADA_TOTAL)
                                    load_ada(a, j)
                for j in range(4):
                    load_w(w0 + UNITS - 4 + j, j)
                with sp.If(l < DEPTH - 1):
                    for j in range(2):
                        load_w(within(w0 + UNITS + j, DEPTH * UNITS), j)
                        for k in range(2):
                            load_ada(within(a0 + 4 * (ADA_STEP - 1) + 2 * j + k, 4 * ADA_TOTAL), k)
            for q in range(4):
                if q < 3:
                    sp.wait_ge(x_first, 3 * 2 * DEPTH + q + 1)
                else:
                    sp.wait_ge(x_last, 2 * DEPTH + 1)
                sp.dma_start(y_t[:, 4 * q:4 * q + 4, :], x[:, 4 * q:4 * q + 4, :]).then_inc(y_saved, 16)
            sp.wait_ge(y_saved, 16 * 4)
            for s in v_saved:
                sp.wait_ge(s, 16 * (DEPTH * HA // 2))
            sp.wait_ge(mix_saved, 16 * DEPTH)
            sp.wait_ge(ffn_saved, 16 * DEPTH * G)

        @block.gpsimd
        def _(pool):
            pool.memset(ones[:, :], 1.0).then_inc(made, 1)
            pool.memset(minus_half[:, :], -0.5).then_inc(made, 1)
            pool.memset(c_act[:, :, :], 0.0).then_inc(made, 1)
            pool.memset(pad[:, :, 0:2], 0.0).then_inc(made, 1)
            pool.sem_inc(v_free, 2)
            pool.sem_inc(sq_added, 1)
            pool.sem_inc(pad_kept, 2)
            pool.sem_inc(x_last, 1)

            def reset_sums(n):
                pool.memset(sq_sum[:, :, :], 0.0).then_inc(sq_reset, 1)
                pool.wait_ge(sq_reset, n)
                apart(pool)

            def add_square(l, k, source, which):
                pool.wait_ge(sq_added, SQUARES * l + k + 1)
                pool.tensor_tensor(sq[:, :], source, source, ALU.mult).then_inc(sq_one, 1)
                pool.wait_ge(sq_one, SQUARES * l + k + 1)
                pool.tensor_tensor(sq_sum[:, which, :], sq_sum[:, which, :], sq[:, :], ALU.add)\
                    .then_inc(sq_added, 1)

            def root(l, k):
                pool.wait_ge(norm_var, CHAINS * l + k + 1)
                pool.tensor_tensor(rstd[:, :], var[:, :], minus_half[:, :], ALU.pow).then_inc(norm_rstd, 1)

            def fill_history(w, slot, source):
                pool.wait_ge(conv_done, w + 1)
                apart(pool)
                pool.tensor_copy(padded(pad[:, slot, :], 0, 2), source).then_inc(pad_hist, 1)

            def keep_last(slot, target):
                apart(pool)
                pool.tensor_copy(target[:, 0, :], pad[:, slot, SEQ:S0])
                pool.tensor_copy(target[:, 1:R, :], padded(pad[:, slot, :], STEP, 2)).then_inc(pad_kept, 1)

            def load_history(l, g):
                pool.dma_start(ffn_old[:, :, :, :].rearrange("p b s t -> p (b s t)"), ffn_hist[l, g])\
                    .then_inc(hist_landed, 16)

            def update_last(l, e):
                n = 2 * l + e
                quarter = slice(12, 16)
                pool.wait_ge(rows_last, n + 1)
                pool.wait_ge(gated_prompt, 16 * n + 16)
                pool.wait_ge(gated_sample, 4 * n + 4)
                rows = over_blocks(diag[:, 1, :], 4)
                pool.tensor_tensor(stage[:, quarter, :], stage[:, quarter, :], rows, ALU.mult)\
                    .then_inc(scaled_last, 1)
                pool.wait_ge(scaled_last, n + 1)
                pool.tensor_tensor(x[:, quarter, :], x[:, quarter, :], stage[:, quarter, :], ALU.add)\
                    .then_inc(x_last, 1)

            def modulate_rest(l, e):
                pool.wait_ge(coef_ready, 4 * l + 2 * e + 1)
                for q in range(4):
                    n = 8 * l + 4 * e + q
                    b = 4 * q + 3
                    pool.wait_ge(x_scaled, n + 1)
                    apart(pool)
                    pool.tensor_scalar(stage[:, b, 0:SEQ], stage[:, b, 0:SEQ], coef_scale[:, b, 0:1],
                                       coef_shift[:, b, 0:1], ALU.mult, ALU.add)
                    pool.tensor_tensor(quarter_samples(stage, q), quarter_samples(stage, q),
                                       per_sample(coef_scale, q), ALU.mult).then_inc(h_sample, 1)
                    pool.wait_ge(h_sample, 2 * n + 1)
                    pool.tensor_tensor(quarter_samples(stage, q), quarter_samples(stage, q),
                                       per_sample(coef_shift, q), ALU.add).then_inc(h_sample, 1)

            pool.wait_ge(made, 4)
            root(0, 0)
            with pool.Fori(0, DEPTH) as l:
                b0 = BLOCKS * l
                pool.wait_ge(blocks_done, b0 + 1)
                pool.wait_ge(c_ready, 1)
                pool.dma_start(sp_w[:, :], w_sp[l]).then_inc(mix_landed, 16)
                pool.dma_start(sp_ws[:, :], w_sp_s[l]).then_inc(mix_landed, 16)
                pool.dma_start(sp_b[0:1, :], b_sp[l]).then_inc(mix_landed, 16)
                pool.dma_start(mix_old[:, :, :, :].rearrange("p b s t -> p (b s t)"), mix_hist[l])\
                    .then_inc(mix_landed, 16)
                modulate_rest(l, 0)
                pool.wait_ge(mix_landed, 64 * l + 64)
                apart(pool)
                wp = sp_w[:, :].rearrange("p (h t) -> p h t", t=P)
                pool.affine_select(out=wp, in_=wp, compare_op=ALU.is_ge, fill=0.0, base=0,
                                   pattern=[[0, HA], [1, P]], channel_multiplier=-1).then_inc(masked, 1)
                ws = sp_ws[:, :].rearrange("p (h t) -> p h t", h=HA)
                pool.affine_select(out=ws, in_=ws, compare_op=ALU.is_ge, fill=0.0, base=0,
                                   pattern=[[0, HA], [1, SEQS * STEP]], channel_multiplier=-1)\
                    .then_inc(masked, 1)
                reset_sums(4 * l + 1)
                with pool.Fori(0, HA // 4) as i:
                    for jj in range(4):
                        pool.wait_ge(taken[jj % 2], BLOCKS // 2 * l + 2 * i + jj // 2 + 2)
                        add_square(l, 4 * i + jj, stage[:, 4 * i + jj, :], 0)
                root(l, 1)
                reset_sums(4 * l + 2)
                with pool.Fori(0, HB // 4) as i:
                    for jj in range(4):
                        j = 4 * i + jj
                        w = PADS * l + j
                        fill_history(w, jj % 2, mix_old[:, j, :, :])
                        pool.wait_ge(v_normed, HA * l + j + 1)
                        pool.dma_start(v_rows[l, j], v_norm[:, jj % 2, P:T]).then_inc(v_saved[jj % 2], 16)
                        bh = HA + 3 * jj + 1
                        pool.wait_ge(taken[bh % 2], BLOCKS // 2 * l + 6 * i + bh // 2 + 2)
                        keep_last(jj % 2, mix_new[:, j, :, :])
                        bb = bh + 1
                        pool.wait_ge(taken[bb % 2], BLOCKS // 2 * l + 6 * i + bb // 2 + 2)
                        add_square(l, HA + j, stage[:, HA + j, :], 1)
                        pool.wait_ge(v_saved[jj % 2], 16 * (HA // 2 * l + 2 * i + jj // 2 + 1))
                        pool.sem_inc(v_free, 1)
                pool.wait_ge(pad_kept, PADS * l + HB + 2)
                pool.dma_start(new_mix[l], mix_new[:, :, :, :].rearrange("p b s t -> p (b s t)"))\
                    .then_inc(mix_saved, 16)
                for j in range(HA):
                    pool.wait_ge(a_ready, HA * l + j + 2)
                    add_square(l, HA + HB + j, stage[:, j, :], 0)
                    if j == 1:
                        root(l, 2)
                root(l, 3)
                pool.wait_ge(mix_saved, 16 * l + 16)
                pool.wait_ge(a_ready, HA * l + HA + 1)
                load_history(l, 0)
                reset_sums(4 * l + 3)
                with pool.Fori(0, KD // 4) as i:
                    for jj in range(4):
                        b = A_UNITS - KD + jj
                        pool.wait_ge(taken[b % 2], BLOCKS // 2 * l + 2 * i + b // 2 + 2)
                        add_square(l, 2 * HA + HB + 4 * i + jj, stage[:, 4 * i + jj, :], 0)
                root(l, 4)
                update_last(l, 0)
                root(l, 5)
                modulate_rest(l, 1)
                pool.wait_ge(h_ready, 12 * l + 12)
                apart(pool)
                pool.memset(stage[:, :, :], 0.0).then_inc(zeroed, 1)
                reset_sums(4 * l + 4)

                def group_states(l, g, half, first=False, last=False):
                    pool.wait_ge(hist_landed, 16 * (G * l + g + 1))
                    for n in range(8):
                        w = PADS * l + HB + 8 * g + n
                        fill_history(w, n % 2, ffn_old[:, n, :, :])
                        if n == 7 and not last:
                            pool.wait_ge(pad_hist, w + 1)
                            load_history(l, g + 1)
                        if n == 0 and not first:
                            pool.wait_ge(ffn_saved, 16 * (G * l + g))
                        pool.wait_ge(taken[n % 2], BLOCKS // 2 * l + half(n) + 2)
                        keep_last(n % 2, ffn_new[:, n, :, :])
                    pool.wait_ge(pad_kept, PADS * l + HB + 8 * g + 10)
                    pool.dma_start(new_ffn[l, g], ffn_new[:, :, :, :].rearrange("p b s t -> p (b s t)"))\
                        .then_inc(ffn_saved, 16)

                def half_block(g):
                    first = A_BLOCKS // 2 + 4 + (4 + KD // 2) * (g - 1)
                    return lambda n: first + (n if n < 2 else n + KD) // 2

                group_states(l, 0, lambda n: (A_BLOCKS + n) // 2, first=True)
                with pool.Fori(1, G - 1) as g:
                    group_states(l, g, half_block(g))
                group_states(l, G - 1, half_block(G - 1), last=True)
                with pool.Fori(0, KD // 4) as i:
                    for jj in range(4):
                        b = BLOCKS - KD + jj
                        pool.wait_ge(taken[b % 2], BLOCKS // 2 * l + 2 * i + b // 2 + 2)
                        add_square(l, SQUARES - KD + 4 * i + jj, stage[:, 4 * i + jj, :], 0)
                root(l, 6)
                update_last(l, 1)
                with pool.If(l < DEPTH - 1):
                    root(l, CHAINS)
                pool.wait_ge(ffn_saved, 16 * G * (l + 1))
                apart(pool)

        @block.tensor
        def _(pe):
            pe.sem_inc(blocks_done, 1)
            pe.sem_inc(ada_turned, 1)

            def split_ready(u):
                pe.wait_ge(split_done, RAW + u + 1)

            def bank_free(l, half, bank):
                pe.wait_ge(taken[bank], BLOCKS // 2 * l + half + 1)

            def three(out, hi, lo, k, moving_hi, moving_lo, first, last):
                pe.matmul(out, hi, moving_hi[:, k, :], start=first, stop=False)
                pe.matmul(out, hi, moving_lo[:, k, :], start=False, stop=False)
                return pe.matmul(out, lo, moving_hi[:, k, :], start=False, stop=last)

            def unit_block(l, u, half, slot, bank, h_from=None, order=range(4), spread_in=None):
                split_ready(UNITS * l + u)
                bank_free(l, half, bank)
                for n, q in enumerate(order):
                    if n == 2 and spread_in is not None:
                        with pe.If(spread_in < 1):
                            spread(l, 3)
                    if h_from is not None:
                        pe.wait_ge(h_ready, h_from + n + 1)
                    for k in range(4 * q, 4 * q + 4):
                        cols = slice(k * P, (k + 1) * P)
                        mm = three(main[bank][:, 0:T], w_hi[:, slot, cols], w_lo[:, slot, cols], k, h_hi, h_lo,
                                   n == 0 and k == 4 * q, n == 3 and k == 4 * q + 3)
                mm.then_inc(blocks_done, 1)

            def down_unit(l, u, half, slot):
                split_ready(UNITS * l + u)
                for m in range(4):
                    bank_free(l, half + m // 2, m % 2)
                    for k in range(4):
                        cols = slice(k * 512 + m * P, k * 512 + (m + 1) * P)
                        mm = three(main[m % 2][:, 0:T], w_hi[:, slot, cols], w_lo[:, slot, cols], k, ff_hi,
                                   ff_lo, k == 0, k == 3)
                    mm.then_inc(blocks_done, 1)

            def ada_unit(kk, weights):
                for j in range(4):
                    mm = pe.matmul(ada_acc[32 * j:32 * j + 32, :], c_act[:, 4 * kk + j, :], weights[:, j, :],
                                   start=(kk == 0), stop=(kk == 3))
                mm.then_inc(ada_used, 1)

            def ada_ahead(c):
                pe.wait_ge(ada_out, c + 1)
                for kk in range(4):
                    pe.wait_ge(ahead_landed[kk], 16 * (c + 1))
                    ada_unit(kk, ahead_buffer(kk))

            def ahead_chunks(first, end):
                with pe.Fori(first, end) as c:
                    ada_ahead(c)
                    ada_turn(c)

            def ada_part(c, parts):
                for kk in parts:
                    if kk == 0:
                        pe.wait_ge(ada_out, c + 1)
                    pe.wait_ge(ada_landed[kk % 2], 16 * (2 * (c - ADA_AHEAD) + kk // 2 + 1))
                    ada_unit(kk, ada_raw[:, kk % 2, :, :])

            def ada_turn(c):
                pe.wait_ge(ada_out, c + 2)
                pe.wait_ge(mod_ready, c + 1)
                for b in range(4):
                    mm = pe.matmul(ada_t[:, b, :], ada_sum[:, b * P:(b + 1) * P], select, start=True, stop=True)
                mm.then_inc(ada_turned, 1)

            def spread(l, k, which=0):
                pe.wait_ge(norm_diag, CHAINS * l + k + 1)
                pe.matmul(rb[which][:, 0:T], ones[:, :], diag[:, which, :], start=True, stop=True)\
                    .then_inc(norm_rb, 1)

            def spread_last():
                pe.matmul(rb[1][:, 0:T], ones[:, :], diag[:, 0, :], start=True, stop=True)\
                    .then_inc(norm_rb_last, 1)

            def sum_squares(l, squares, which=0):
                pe.wait_ge(sq_added, SQUARES * l + squares + 1)
                for t, first in enumerate((0, P, T - P)):
                    mm = pe.matmul(stat[:, t:t + 1], sq_sum[:, which, first:first + P], ones[:, 0:1],
                                   start=(t == 0), stop=True, skip_group_check=True)
                mm.then_inc(norm_sum, 1)

            def x_root(n, beside_first=None, beside_second=None):
                for i, q in enumerate(UPDATE_ORDER):
                    pe.wait_ge(x_squares, 4 * n + i + 1)
                    for j in range(4):
                        mm = pe.matmul(mixed[32 * j:32 * j + 32, 0:T], ones[:, 0:32], stage[:, 4 * q + j, :],
                                       start=(i == 0), stop=(i == 3))
                    if i == 3:
                        mm.then_inc(x_summed, 1)
                    if i == 0 and beside_first is not None:
                        beside_first()
                    if i == 1 and beside_second is not None:
                        beside_second()
                pe.wait_ge(x_copied, n + 1)
                for t, first in enumerate((0, P, T - P)):
                    mm = pe.matmul(stat[:, t:t + 1], diag[:, 1, first:first + P], select[:, 0:1],
                                   start=(t == 0), stop=True, skip_group_check=True)
                mm.then_inc(norm_sum, 1)

            def mid_second(l, c, parts):
                with pe.If(l < DEPTH - 1):
                    ada_part(c, parts)

            def turn_v(l, j, slot):
                pe.wait_ge(v_normed, HA * l + j + 1)
                pe.wait_ge(v_tokens, HA * l + j + 1)
                for t, n in enumerate((P, P, T - SEQ)):
                    mm = pe.transpose(tok[0:n, t * P:(t + 1) * P], v_norm[:, slot, t * P:t * P + n], ident)
                mm.then_inc(v_turned, 1)

            def mix(l, j, slot):
                pe.wait_ge(v_tokens, HA * l + j + 2)
                pe.wait_ge(mixed_out, HA * l + j + 1)
                bias = sp_b[0:1, bass.ds(j * P, P)]
                for chunk in range(2):
                    cols = slice(chunk * P, (chunk + 1) * P)
                    pe.matmul(mixed[:, cols], v_tok[:, slot, cols], sp_w[:, bass.ds(j * P, P)],
                              start=(chunk == 0), stop=False, skip_group_check=True)
                    pe.matmul(mixed[:, cols], ones[0:1, :], bias, start=False, stop=False, skip_group_check=True)
                n = SEQS * STEP
                pe.matmul(mixed[:, SEQ:T], v_tok[0:n, slot, 2 * P:3 * P], sp_ws[0:n, bass.ds(j * n, n)],
                          start=False, stop=False, skip_group_check=True)
                pe.matmul(samples(mixed), ones[0:1, :],
                          sp_b[0:1, bass.ds(j * P, STEP)].unsqueeze(1).broadcast_to([1, SEQS, STEP]),
                          start=False, stop=True, skip_group_check=True).then_inc(mix_done, 1)

            def beside(c, unit):
                if unit == 3:
                    ada_turn(c)
                else:
                    ada_part(c, [(0,), (1,), (2, 3)][unit])

            pe.wait_ge(c_loaded, 16 * 2)
            pe.wait_ge(made, 4)
            pe.wait_ge(c_ready, 1)
            ahead_chunks(0, ADA_AHEAD // 2)
            x_root(0)
            spread(0, 0)
            ahead_chunks(ADA_AHEAD // 2, ADA_AHEAD)
            with pe.Fori(0, DEPTH) as l:
                c0 = ADA_AHEAD + ADA_STEP * l
                with pe.Fori(0, HA // 4) as i:
                    for j in range(4):
                        unit_block(l, 4 * i + j, 2 * i + j // 2, j % 2, j % 2, 12 * l if j == 0 else None)
                        beside(c0 + i, j)
                sum_squares(l, HA)
                spread(l, 1)
                pe.wait_ge(masked, 2 * l + 2)
                apart(pe)
                with pe.Fori(0, HB // 4) as i:
                    for jj in range(4):
                        for m in range(3):
                            n = 3 * jj + m
                            unit_block(l, HA + 12 * i + n, 6 * i + (HA + n) // 2, n % 2, n % 2)
                            beside(c0 + 2 + 3 * i + n // 4, n % 4)
                            if m == 1:
                                turn_v(l, 4 * i + jj, jj % 2)
                            if m == 2:
                                mix(l, 4 * i + jj, jj % 2)
                for j in range(HA):
                    unit_block(l, U_UNIT + j, (U_UNIT + j) // 2, j % 2, j % 2)
                    beside(c0 + 8 + j // 4, j % 4)
                    if j == 1:
                        sum_squares(l, HA + HB, 1)
                    if j == 2:
                        spread(l, 2, 1)
                sum_squares(l, 2 * HA + HB)
                with pe.Fori(0, KD // 4) as i:
                    for j in range(4):
                        unit_block(l, OUT_UNIT + 4 * i + j, OUT_UNIT // 2 + 2 * i + j // 2, j % 2, j % 2,
                                   12 * l + 4 if j == 0 else None, OUT_ORDER, i if j == 0 else None)
                        beside(c0 + 10 + i, j)
                c = c0 + ADA_A
                ada_part(c, (0,))
                sum_squares(l, 2 * HA + HB + KD)
                ada_part(c, (1,))
                spread(l, 4)
                spread_last()
                ada_part(c, (2, 3))
                x_root(2 * l + 1, lambda: ada_turn(c), lambda: mid_second(l, c + 1, (0,)))
                mid_second(l, c + 1, (1,))
                spread(l, 5)
                mid_second(l, c + 1, (2, 3))
                for n in range(8):
                    unit_block(l, A_UNITS + n, (A_BLOCKS + n) // 2, n % 2, n % 2, 12 * l + 8 if n == 0 else None)
                    if n == 0:
                        with pe.If(l < DEPTH - 1):
                            ada_turn(c + 1)
                with pe.Fori(0, G - 1) as g:
                    u0 = A_UNITS + 8 + 12 * g
                    half = A_BLOCKS // 2 + 4 + (4 + KD // 2) * g
                    c = ffn_chunk(l, g)
                    for n in range(2):
                        unit_block(l, u0 + n, half + n // 2, n % 2, n % 2)
                    with pe.If(c < ADA_CHUNKS + ADA_AHEAD):
                        ada_part(c, (0, 1))
                    pe.wait_ge(ff_ready, 4 * G * l + 4 * g + 4)
                    for n in range(4):
                        down_unit(l, u0 + 2 + n, half + 1 + 2 * n, n % 2)
                    with pe.If(c < ADA_CHUNKS + ADA_AHEAD):
                        ada_part(c, (2, 3))
                    for n in range(2, 8):
                        unit_block(l, u0 + 4 + n, half + (KD + n) // 2, n % 2, n % 2)
                        if n == 3:
                            with pe.If(c < ADA_CHUNKS + ADA_AHEAD):
                                ada_turn(c)
                pe.wait_ge(ff_ready, 4 * G * l + 4 * G)
                for n in range(4):
                    down_unit(l, UNITS - 4 + n, (BLOCKS - KD) // 2 + 2 * n, n % 2)
                c = c0 + ADA_STEP - 1
                with pe.If(l < DEPTH - 1):
                    ada_part(c, (0,))
                sum_squares(l, SQUARES)
                with pe.If(l < DEPTH - 1):
                    ada_part(c, (1,))
                spread(l, 6)
                spread_last()
                with pe.If(l < DEPTH - 1):
                    ada_part(c, (2, 3))
                    x_root(2 * l + 2, lambda: ada_turn(c))
                    spread(l, CHAINS)

        @block.scalar
        def _(act):
            act.dma_start(c_raw[:, :, :], c_t).then_inc(c_loaded, 16)
            act.dma_start(cst[:, :], consts).then_inc(c_loaded, 16)
            act.dma_start(b_ada[:, :], b_ada_t).then_inc(loaded, 16)
            act.dma_start(x[:, :, :], x_t).then_inc(loaded, 16)
            act.dma_start(par[:, :].rearrange("p (l n) -> p l n", l=DEPTH), params.rearrange("l p n -> p l n"))\
                .then_inc(loaded, 16)
            act.sem_inc(ada_out, 1)
            act.sem_inc(v_tokens, 1)
            act.sem_inc(mixed_out, 1)
            act.wait_ge(c_loaded, 16 * 2)
            act.wait_ge(made, 4)
            act.activation(c_act[:, :, 0:R], c_raw[:, :, :], ACT.Silu).then_inc(c_ready, 1)

            def split_hi(l, u, slot, landing):
                act.wait_ge(w_landed[slot], 16 * (UNITS // RAW * l + landing + 1))
                act.activation(w_hi[:, slot % 2, :], w_raw[:, slot, :], ACT.Copy).then_inc(hi_done, 1)

            def next_hi(l, u, blocks, slot, landing):
                act.wait_ge(blocks_done, BLOCKS * l + blocks + 1)
                split_hi(l, u + 1, slot, landing)

            def take_chunk(c):
                act.wait_ge(ada_used, 4 * c + 4)
                act.wait_ge(ada_turned, c + 1)
                act.activation(ada_sum[:, :], ada_acc[:, :], ACT.Copy).then_inc(ada_out, 1)

            def block_ready(l, b):
                act.wait_ge(blocks_done, BLOCKS * l + b + 2)

            def square_x(n, chunk=None):
                for q in UPDATE_ORDER:
                    if q < 3:
                        act.wait_ge(x_first, 3 * n + q + 1)
                    else:
                        act.wait_ge(x_last, n + 1)
                    act.activation(stage[:, 4 * q:4 * q + 4, :], x[:, 4 * q:4 * q + 4, :], ACT.Square)\
                        .then_inc(x_squares, 1)
                    if q == 0 and chunk is not None:
                        take_chunk(chunk)

            def copy_rstd(n):
                act.wait_ge(norm_rb_last, n + 1)
                act.activation(diag[:, 1, :], rb[1][:, 0:T], ACT.Copy).then_inc(rows_last, 1)

            def copy_sums(n):
                act.wait_ge(x_summed, n + 1)
                act.activation(diag[:, 1, :], mixed[:, 0:T], ACT.Copy).then_inc(x_copied, 1)

            def hi_quarter(n, q):
                act.activation(h_hi[:, 4 * q:4 * q + 4, :], stage[:, 4 * q:4 * q + 4, :], ACT.Copy)\
                    .then_inc(hi_h, 1)

            def modulate_prompt(l, e):
                act.wait_ge(coef_ready, 4 * l + 2 * e + 1)
                for q in range(4):
                    n = 8 * l + 4 * e + q
                    act.wait_ge(x_scaled, n + 1)
                    for b in range(4 * q, 4 * q + 3):
                        step = act.activation(stage[:, b, 0:SEQ], stage[:, b, 0:SEQ], ACT.Identity,
                                              scale=coef_scale[:, b, 0:1], bias=coef_shift[:, b, 0:1])
                    step.then_inc(h_prompt, 1)
                    act.wait_ge(h_prompt, n + 1)
                    act.wait_ge(h_sample, 2 * n + 2)
                    hi_quarter(n, q)

            def gate_prompt(l, e, b):
                squares = SQUARES * l + (2 * HA + HB if e == 0 else SQUARES - KD)
                act.wait_ge(sq_one, squares + b + 1)
                act.activation(stage[:, b, 0:SEQ], stage[:, b, 0:SEQ], ACT.Identity,
                               scale=coef_gate[:, bass.ds(b, 1), 0]).then_inc(gated_prompt, 1)

            def first_tap(w, slot, out, column, bias):
                act.wait_ge(pad_hist, w + 1)
                act.activation(out, pad[:, slot, 2:PAD], ACT.Identity, scale=column(2), bias=bias)\
                    .then_inc(tap2, 1)

            with act.Fori(0, ADA_AHEAD // 2) as c:
                take_chunk(c)
            act.wait_ge(loaded, 16 * 3)
            square_x(0)
            copy_sums(0)
            split_hi(0, 0, 0, 0)
            split_hi(0, 1, 1, 0)
            with act.Fori(ADA_AHEAD // 2, ADA_AHEAD) as c:
                take_chunk(c)
            with act.Fori(0, DEPTH) as l:
                c0 = ADA_AHEAD + ADA_STEP * l
                act.activation(warm[:, 0:1], cst[:, 0:1], ACT.Gelu_apprx_tanh)
                modulate_prompt(l, 0)
                with act.Fori(0, HA // 4) as i:
                    for j in range(4):
                        u = 4 * i + j
                        if j == 0:
                            with act.If(i > 0):
                                next_hi(l, u, u, 1, i)
                        else:
                            next_hi(l, u, u, (j + 1) % RAW, i + (j + 1) // 4)
                        block_ready(l, u)
                        act.activation(stage[:, u, :], main[j % 2][:, 0:T], ACT.Gelu_apprx_tanh)\
                            .then_inc(taken[j % 2], 1)
                        if j == 2:
                            take_chunk(c0 + i)
                with act.Fori(0, HB // 4) as i:
                    for jj in range(4):
                        j = 4 * i + jj
                        w = PADS * l + j
                        for m in range(3):
                            n = 3 * jj + m
                            u = HA + 12 * i + n
                            next_hi(l, u, u, (n + 1) % RAW, 2 + 3 * i + (n + 1) // 4)
                            if m == 0:
                                block_ready(l, u)
                                act.activation(gate_c[:, :], main[n % 2][:, 0:T], ACT.Copy)\
                                    .then_inc(taken[n % 2], 1)
                            if m == 1:
                                act.wait_ge(taken[n % 2], BLOCKS // 2 * l + 6 * i + (HA + n) // 2 + 2)
                                first_tap(w, jj % 2, conv_mix[:, :], lambda t: pcol(l, W_MIX + 3 * j + t), 0.0)
                                act.wait_ge(v_turned, HA * l + j + 1)
                                act.activation(v_tok[:, jj % 2, 0:SEQ], tok[:, 0:SEQ], ACT.Copy)
                                act.activation(v_tok[0:T - SEQ, jj % 2, SEQ:], tok[0:T - SEQ, SEQ:3 * P],
                                               ACT.Copy).then_inc(v_tokens, 1)
                            if m == 2:
                                act.wait_ge(mix_done, HA * l + j + 1)
                                act.activation(stage[:, j, :], mixed[:, 0:T], ACT.Copy).then_inc(mixed_out, 1)
                            if n % 4 == 2:
                                take_chunk(c0 + 2 + 3 * i + n // 4)
                for j in range(HA):
                    u = U_UNIT + j
                    next_hi(l, u, u, (j + 1) % RAW, (u + 1) // RAW)
                    block_ready(l, u)
                    act.wait_ge(a_ready, HA * l + j + 1)
                    act.activation(u_act[:, :], main[j % 2][:, 0:T], ACT.Gelu_apprx_tanh).then_inc(taken[j % 2], 1)
                    if j % 4 == 2:
                        take_chunk(c0 + 8 + j // 4)
                for n, q in enumerate(OUT_ORDER):
                    act.wait_ge(ab_scaled, 4 * l + n + 1)
                    hi_quarter(12 * l + 4 + n, q)
                act.wait_ge(coef_ready, 4 * l + 2)
                with act.Fori(0, KD // 4) as i:
                    for j in range(4):
                        u = OUT_UNIT + 4 * i + j
                        next_hi(l, u, u, (j + 1) % RAW, OUT_UNIT // RAW + i + (j + 1) // RAW)
                        block_ready(l, u)
                        act.activation(stage[:, 4 * i + j, :], main[j % 2][:, 0:T], ACT.Copy)\
                            .then_inc(taken[j % 2], 1)
                        gate_prompt(l, 0, 4 * i + j)
                        if j == 2:
                            take_chunk(c0 + 10 + i)
                act.activation(warm[:, 1:2], cst[:, 0:1], ACT.Silu)
                next_hi(l, A_UNITS, A_BLOCKS, 1, A_UNITS // RAW)
                copy_rstd(2 * l)
                square_x(2 * l + 1, c0 + ADA_A)
                copy_sums(2 * l + 1)
                modulate_prompt(l, 1)
                with act.If(l < DEPTH - 1):
                    take_chunk(c0 + ADA_A + 1)

                def take_row(l, g, n, b, half):
                    w = PADS * l + HB + 8 * g + n
                    block_ready(l, b)
                    act.wait_ge(conv_done, w + 1)
                    act.wait_ge(pad_kept, w + 1)
                    act.activation(pad[:, n % 2, 2:S0], main[n % 2][:, 0:SEQ], ACT.Copy)
                    act.activation(padded(pad[:, n % 2, :], 2, STEP), samples(main[n % 2]), ACT.Copy)\
                        .then_inc(taken[n % 2], 1)
                    act.wait_ge(taken[n % 2], BLOCKS // 2 * l + half + 2)
                    column = W_CF + 4 * (8 * g + n)
                    first_tap(w, n % 2, conv_ffn[:, n % 2, :], lambda t: pcol(l, column + t), pcol(l, column + 3))

                def gate(l, g, pair):
                    act.wait_ge(conv_done, PADS * l + HB + 8 * g + 2 * pair + 3)
                    act.activation(gate_act[:, :], conv_ffn[:, 0, :], ACT.Silu).then_inc(gate_done, 1)

                def ff_hi_part(l, g, pair):
                    act.wait_ge(ff_done, 4 * (G * l + g) + pair + 1)
                    act.activation(ff_hi[:, pair, :], ff[:, :], ACT.Copy).then_inc(ff_hi_done, 1)

                for n in range(8):
                    u = A_UNITS + n
                    if n:
                        next_hi(l, u, A_BLOCKS + n, (n + 1) % RAW, (u + 1) // RAW)
                    if n % 2 == 0 and n:
                        ff_hi_part(l, 0, n // 2 - 1)
                    take_row(l, 0, n, A_BLOCKS + n, (A_BLOCKS + n) // 2)
                    if n % 2:
                        gate(l, 0, n // 2)
                with act.Fori(0, G - 1) as g:
                    u0 = A_UNITS + 8 + 12 * g
                    b0 = A_BLOCKS + 8 + (8 + KD) * g
                    half = A_BLOCKS // 2 + 4 + (4 + KD // 2) * g
                    landing = (A_UNITS + 8) // RAW + 3 * g
                    c = ffn_chunk(l, g)
                    for n in range(12):
                        if n < 2:
                            block, row = n, n
                        elif n < 6:
                            block, row = 2 + 4 * (n - 2), None
                        else:
                            block, row = n - 4 + KD, n - 4
                        next_hi(l, u0 + n, b0 + block, (n + 1) % RAW, landing + (n + 1) // 4)
                        if n == 0:
                            ff_hi_part(l, g, 3)
                        elif row is not None and row % 2 == 0:
                            ff_hi_part(l, g + 1, row // 2 - 1)
                        if row is not None:
                            take_row(l, g + 1, row, b0 + block, half + block // 2)
                            if row % 2:
                                gate(l, g + 1, row // 2)
                        if n == 6:
                            with act.If(c < ADA_CHUNKS + ADA_AHEAD):
                                take_chunk(c)
                ff_hi_part(l, G - 1, 3)
                act.wait_ge(coef_ready, 4 * l + 4)
                for n in range(3):
                    next_hi(l, UNITS - 4 + n, BLOCKS - KD + 4 * n, n + 1, UNITS // RAW - 1)
                    if n:
                        for b in range(4 * n - 4, 4 * n):
                            gate_prompt(l, 1, b)
                with act.If(l < DEPTH - 1):
                    next_hi(l, UNITS - 1, BLOCKS - 4, 0, UNITS // RAW)
                for b in range(8, KD):
                    gate_prompt(l, 1, b)
                with act.If(l < DEPTH - 1):
                    next_hi(l + 1, 0, 0, 1, 0)
                copy_rstd(2 * l + 1)
                with act.If(l < DEPTH - 1):
                    square_x(2 * l + 2, c0 + ADA_STEP - 1)
                    copy_sums(2 * l + 2)

        @block.vector
        def _(dve):
            dve.sem_inc(split_done, RAW)
            for s in taken:
                dve.sem_inc(s, 1)
            dve.sem_inc(mod_ready, 1)
            dve.sem_inc(a_ready, 1)
            dve.sem_inc(conv_done, 2)
            dve.sem_inc(x_first, 3)
            dve.wait_ge(c_loaded, 16 * 2)
            dve.wait_ge(loaded, 16 * 3)

            def split_lo(u, slot):
                dve.wait_ge(hi_done, u + 1)
                dve.tensor_tensor(w_lo[:, slot % 2, :], w_raw[:, slot, :], w_hi[:, slot % 2, :].bitcast(F32),
                                  ALU.subtract).then_inc(split_done, 1)

            def take_mod(c):
                dve.wait_ge(ada_turned, c + 2)
                dve.tensor_tensor(mod[:, bass.ds(4 * c, 4), :], ada_t,
                                  b_ada[:, bass.ds(4 * c, 4)].unsqueeze(2).broadcast_to([P, 4, R]), ALU.add)\
                    .then_inc(mod_ready, 1)

            def mod_of(l, which):
                return mod[:, bass.ds(6 * KD * l + KD * which, KD), :]

            def gains(l, column):
                return par[:, bass.ds(l * NPAR + column, KD)].unsqueeze(2).broadcast_to([P, KD, R])

            def modulation(l, scale, shift, gain, chunks):
                dve.wait_ge(mod_ready, ADA_CHUNKS * l + chunks + 1)
                dve.tensor_copy(coef_shift[:, :, :], mod_of(l, shift))
                dve.scalar_tensor_tensor(coef_scale[:, :, :], mod_of(l, scale), 1.0, gains(l, gain), ALU.add,
                                         ALU.mult).then_inc(coef_ready, 1)

            def gating(l, gate, gain, chunks):
                dve.wait_ge(mod_ready, ADA_CHUNKS * l + chunks + 1)
                dve.tensor_tensor(coef_gate[:, :, :], mod_of(l, gate), gains(l, gain), ALU.mult)\
                    .then_inc(coef_ready, 1)

            def mean(l, k, width):
                dve.wait_ge(norm_sum, CHAINS * l + k + 1)
                dve.tensor_scalar(var[:, :], stat, 1.0 / width, EPS, ALU.mult, ALU.add).then_inc(norm_var, 1)

            def diagonal(l, k, which=0):
                dve.wait_ge(norm_rstd, CHAINS * l + k + 1)
                dve.tensor_scalar(diag[:, which, 0:P], ident, rstd[:, 0:1], None, ALU.mult)
                dve.tensor_scalar(diag[:, which, P:2 * P], ident, rstd[:, 1:2], None, ALU.mult)
                dve.tensor_scalar(diag[:, which, SEQ:T], ident[:, P - (T - SEQ):P], rstd[:, 2:3], None, ALU.mult)\
                    .then_inc(norm_diag, 1)

            def spread_done(l, k):
                dve.wait_ge(norm_rb, CHAINS * l + k + 1)
                apart(dve)

            def root(l, k, width):
                mean(l, k, width)
                diagonal(l, k)
                spread_done(l, k)

            def lo_quarter(n, q):
                dve.wait_ge(hi_h, n + 1)
                quarter = slice(4 * q, 4 * q + 4)
                dve.tensor_tensor(h_lo[:, quarter, :], stage[:, quarter, :], h_hi[:, quarter, :].bitcast(F32),
                                  ALU.subtract).then_inc(h_ready, 1)

            def normed_h(l, e, n):
                for q in range(6):
                    if q < 4:
                        quarter = slice(4 * q, 4 * q + 4)
                        dve.tensor_tensor(stage[:, quarter, :], x[:, quarter, :], over_blocks(rb[0], 4), ALU.mult)\
                            .then_inc(x_scaled, 1)
                    if q > 1:
                        lo_quarter(12 * l + n + q - 2, q - 2)

            def gate_samples(l, e, q):
                squares = SQUARES * l + (2 * HA + HB if e == 0 else SQUARES - KD)
                dve.wait_ge(sq_one, squares + 4 * q + 4)
                rows = stage[:, bass.ds(4 * q, 4), SEQ:T].rearrange("p b (s t) -> p b s t", t=STEP)
                gates = coef_gate[:, bass.ds(4 * q, 4), 1:R].unsqueeze(3).broadcast_to([P, 4, SEQS, STEP])
                dve.tensor_tensor(rows, rows, gates, ALU.mult).then_inc(gated_sample, 1)

            def update_x(l, e):
                n = 2 * l + e
                for q in range(3):
                    quarter = slice(4 * q, 4 * q + 4)
                    dve.wait_ge(gated_prompt, 16 * n + 4 * q + 4)
                    dve.wait_ge(gated_sample, 4 * n + q + 1)
                    dve.tensor_tensor(stage[:, quarter, :], stage[:, quarter, :], over_blocks(rb[0], 4), ALU.mult)\
                        .then_inc(scaled_first, 1)
                    dve.wait_ge(scaled_first, 3 * n + q + 1)
                    dve.tensor_tensor(x[:, quarter, :], x[:, quarter, :], stage[:, quarter, :], ALU.add)\
                        .then_inc(x_first, 1)

            def other_taps(w, slot, row, column):
                dve.wait_ge(tap2, w + 1)
                dve.scalar_tensor_tensor(row, pad[:, slot, 1:PAD - 1], column(1), row, ALU.mult, ALU.add)\
                    .then_inc(tap1, 1)
                dve.wait_ge(tap1, w + 1)
                dve.scalar_tensor_tensor(row, pad[:, slot, 0:PAD - 2], column(0), row, ALU.mult, ALU.add)\
                    .then_inc(conv_done, 1)

            def block_ready(l, b):
                dve.wait_ge(blocks_done, BLOCKS * l + b + 2)

            with dve.Fori(0, ADA_AHEAD // 2) as c:
                take_mod(c)
            root(0, 0, D_MODEL)
            split_lo(0, 0)
            split_lo(1, 1)
            with dve.Fori(ADA_AHEAD // 2, ADA_AHEAD) as c:
                take_mod(c)
            modulation(0, SCALE1, SHIFT1, G_PRE_MIX, 8)
            with dve.Fori(0, DEPTH) as l:
                u0 = UNITS * l
                c0 = ADA_AHEAD + ADA_STEP * l
                normed_h(l, 0, 0)
                with dve.Fori(0, HA // 4) as i:
                    for j in range(4):
                        if j == 0:
                            with dve.If(i > 0):
                                split_lo(u0 + 4 * i + 1, 1)
                        else:
                            split_lo(u0 + 4 * i + j + 1, (j + 1) % RAW)
                    take_mod(c0 + i)
                root(l, 1, W_A)
                with dve.Fori(0, HB // 4) as i:
                    for jj in range(4):
                        j = 4 * i + jj
                        w = PADS * l + j
                        for m in range(3):
                            n = 3 * jj + m
                            u = HA + 12 * i + n
                            split_lo(u0 + u + 1, (n + 1) % RAW)
                            bank = main[n % 2]
                            half = BLOCKS // 2 * l + 6 * i + (HA + n) // 2 + 2
                            if m == 0:
                                dve.wait_ge(v_free, HA * l + j + 1)
                                dve.wait_ge(v_tokens, HA * l + j + 1)
                                dve.scalar_tensor_tensor(v_norm[:, jj % 2, :], stage[:, j, :], pcol(l, G_V + j),
                                                         rb[0][:, 0:T], ALU.mult, ALU.mult).then_inc(v_normed, 1)
                            if m == 1:
                                block_ready(l, u)
                                dve.wait_ge(taken[(n - 1) % 2], BLOCKS // 2 * l + 6 * i + (HA + n - 1) // 2 + 2)
                                dve.wait_ge(pad_kept, w + 1)
                                row = pad[:, jj % 2, :]
                                dve.tensor_tensor(row[:, 2:S0], gate_c[:, 0:SEQ], bank[:, 0:SEQ], ALU.mult)
                                dve.tensor_tensor(padded(row, 2, STEP), samples(gate_c), samples(bank), ALU.mult)\
                                    .then_inc(taken[n % 2], 1)
                                other_taps(w, jj % 2, conv_mix[:, :], lambda t: pcol(l, W_MIX + 3 * j + t))
                            if m == 2:
                                block_ready(l, u)
                                dve.wait_ge(conv_done, w + 3)
                                dve.tensor_tensor(stage[:, HA + j, 0:SEQ], conv_mix[:, 0:SEQ], bank[:, 0:SEQ],
                                                  ALU.mult)
                                dve.tensor_tensor(samples(stage[:, HA + j, :]), conv_samples(conv_mix),
                                                  samples(bank), ALU.mult).then_inc(taken[n % 2], 1)
                            if n % 4 == 3:
                                take_mod(c0 + 2 + 3 * i + n // 4)
                def scale_ab(blocks):
                    for b in blocks:
                        step = dve.scalar_tensor_tensor(stage[:, b, :], stage[:, b, :], pcol(l, G_OUT + b),
                                                        rb[b // HA][:, 0:T], ALU.mult, ALU.mult)
                    step.then_inc(ab_scaled, 1)

                for j in range(HA):
                    split_lo(u0 + U_UNIT + j + 1, (j + 1) % RAW)
                    dve.wait_ge(taken[j % 2], BLOCKS // 2 * l + (U_UNIT + j) // 2 + 2)
                    dve.wait_ge(mixed_out, HA * l + j + 2)
                    dve.tensor_tensor(stage[:, j, :], stage[:, j, :], u_act[:, :], ALU.mult).then_inc(a_ready, 1)
                    if j % 4 == 3:
                        take_mod(c0 + 8 + j // 4)
                    if j == 1:
                        mean(l, 2, W_B)
                        diagonal(l, 2, 1)
                    if j == 3:
                        spread_done(l, 2)
                        scale_ab(range(8, 12))
                    if j == 4:
                        scale_ab(range(12, 16))
                gating(l, GATE1, G_POST_MIX, 12)
                lo_quarter(12 * l + 4, 2)
                mean(l, 3, W_A)
                lo_quarter(12 * l + 5, 3)
                diagonal(l, 3)
                spread_done(l, 3)
                scale_ab(range(0, 4))
                scale_ab(range(4, 8))
                lo_quarter(12 * l + 6, 0)
                lo_quarter(12 * l + 7, 1)
                with dve.Fori(0, KD // 4) as i:
                    for j in range(4):
                        split_lo(u0 + OUT_UNIT + 4 * i + j + 1, (j + 1) % RAW)
                        if j == 0:
                            with dve.If(i > 0):
                                gate_samples(l, 0, within(i - 1, 3))
                    take_mod(c0 + 10 + i)
                gate_samples(l, 0, 3)
                root(l, 4, D_MODEL)
                update_x(l, 0)
                take_mod(c0 + ADA_A)
                modulation(l, SCALE2, SHIFT2, G_PRE_FFN, 20)
                split_lo(u0 + A_UNITS + 1, 1)
                root(l, 5, D_MODEL)
                normed_h(l, 1, 8)

                def conv_row(l, g, n):
                    column = W_CF + 4 * (8 * g + n)
                    other_taps(PADS * l + HB + 8 * g + n, n % 2, conv_ffn[:, n % 2, :],
                               lambda t: pcol(l, column + t))

                def multiply(l, g, pair):
                    dve.wait_ge(gate_done, 4 * (G * l + g) + pair + 1)
                    dve.wait_ge(conv_done, PADS * l + HB + 8 * g + 2 * pair + 4)
                    dve.tensor_tensor(ff[:, 0:SEQ], gate_act[:, 0:SEQ], conv_ffn[:, 1, 0:SEQ], ALU.mult)
                    dve.tensor_tensor(samples(ff), conv_samples(gate_act), conv_samples(conv_ffn[:, 1, :]),
                                      ALU.mult).then_inc(ff_done, 1)

                def ff_lo_part(l, g, pair):
                    dve.wait_ge(ff_hi_done, 4 * (G * l + g) + pair + 1)
                    dve.tensor_tensor(ff_lo[:, pair, :], ff[:, :], ff_hi[:, pair, :].bitcast(F32), ALU.subtract)\
                        .then_inc(ff_ready, 1)

                def add_down(l, b0, n, first=0, end=4):
                    for m in range(first, end):
                        block_ready(l, b0 + m)
                        dve.tensor_tensor(stage[:, 4 * n + m, :], stage[:, 4 * n + m, :], main[m % 2][:, 0:T],
                                          ALU.add).then_inc(taken[m % 2], 1)

                for n in range(8):
                    if n:
                        split_lo(u0 + A_UNITS + n + 1, (n + 1) % RAW)
                    if n == 1:
                        with dve.If(l < DEPTH - 1):
                            take_mod(within(c0 + ADA_A + 1, ADA_TOTAL))
                    if n % 2 == 0 and n:
                        ff_lo_part(l, 0, n // 2 - 1)
                    conv_row(l, 0, n)
                    if n % 2:
                        multiply(l, 0, n // 2)
                dve.wait_ge(zeroed, l + 1)
                apart(dve)
                with dve.Fori(0, G - 1) as g:
                    b0 = A_BLOCKS + 8 + (8 + KD) * g
                    c = ffn_chunk(l, g)
                    for n in range(12):
                        unit = u0 + A_UNITS + 8 + 12 * g + n + 1
                        if 2 <= n < 6:
                            add_down(l, b0 + 2 + 4 * (n - 2), n - 2, 0, 1)
                            split_lo(unit, (n + 1) % RAW)
                            add_down(l, b0 + 2 + 4 * (n - 2), n - 2, 1, 4)
                            continue
                        split_lo(unit, (n + 1) % RAW)
                        row = n if n < 2 else n - 4
                        if row == 0:
                            ff_lo_part(l, g, 3)
                        elif row % 2 == 0:
                            ff_lo_part(l, g + 1, row // 2 - 1)
                        conv_row(l, g + 1, row)
                        if row % 2:
                            multiply(l, g + 1, row // 2)
                        if n == 8:
                            with dve.If(c < ADA_CHUNKS + ADA_AHEAD):
                                take_mod(within(c, ADA_TOTAL))
                gating(l, GATE2, G_POST_FFN, 24)
                ff_lo_part(l, G - 1, 3)
                for n in range(3):
                    add_down(l, BLOCKS - KD + 4 * n, n, 0, 1)
                    split_lo(u0 + UNITS - 4 + n + 1, n + 1)
                    if n:
                        gate_samples(l, 1, n - 1)
                    add_down(l, BLOCKS - KD + 4 * n, n, 1, 4)
                with dve.If(l < DEPTH - 1):
                    split_lo(u0 + UNITS, 0)
                gate_samples(l, 1, 2)
                add_down(l, BLOCKS - 4, 3)
                gate_samples(l, 1, 3)
                root(l, 6, D_MODEL)
                update_x(l, 1)
                with dve.If(l < DEPTH - 1):
                    take_mod(within(c0 + ADA_STEP - 1, ADA_TOTAL))
                    modulation(within(l + 1, DEPTH), SCALE1, SHIFT1, G_PRE_MIX, 8)
                    split_lo(u0 + UNITS + 1, 1)
                    root(l, CHAINS, D_MODEL)


_OUTS = [
    ("y_t", (P, KD, T)),
    ("new_mix", (DEPTH, P, HB * R * 2)),
    ("new_ffn", (DEPTH, G, P, 8 * R * 2)),
    ("v_rows", (DEPTH, HA, P, T - P)),
]


def kernel(x_prompt, x_sample, state_conv_mix, state_conv_ffn, c_prompt, c_sample,
           w_ada, b_ada, g_pre_mix, g_post_mix, g_pre_ffn, g_post_ffn,
           w_in, g_v, w_spatial, b_spatial, w_conv_mix, g_out_a, g_out_b, w_out,
           w_up, w_conv_ffn, b_conv_ffn, w_down):
    import numpy as np
    import concourse.bacc as bacc
    from concourse.bass_utils import run_bass_kernel_spmd

    f = np.float32

    def by_partition(a):
        a = np.asarray(a)
        return a.reshape(a.shape[0], -1, P).transpose(0, 2, 1)

    tokens = np.concatenate([np.asarray(x_prompt).reshape(SEQ, D_MODEL),
                             np.asarray(x_sample).reshape(SEQS * STEP, D_MODEL)])
    x_t = tokens.reshape(T, KD, P).transpose(2, 1, 0)
    rows = np.concatenate([np.asarray(c_prompt), np.asarray(c_sample)])
    c_t = rows.reshape(R, KD, P).transpose(2, 1, 0)
    select = (np.arange(P)[:, None] % 32 == np.arange(R)[None, :]).astype(f)
    consts = np.concatenate([np.eye(P, dtype=f), select], axis=1)

    def by_pair(a, axis):
        a = np.moveaxis(np.asarray(a), axis, -1)
        a = a.reshape(a.shape[:-1] + (2, 4 * G, P))
        return np.moveaxis(a, -3, -2)

    taps = by_pair(w_conv_ffn, 2).reshape(DEPTH, 3, 8 * G, P)
    bias = by_pair(b_conv_ffn, 1).reshape(DEPTH, 1, 8 * G, P)
    conv_ffn = np.concatenate([taps, bias], axis=1).transpose(0, 3, 2, 1).reshape(DEPTH, P, -1)
    conv_mix = np.asarray(w_conv_mix).reshape(DEPTH, 3, HB, P).transpose(0, 3, 2, 1).reshape(DEPTH, P, -1)
    params = np.concatenate(
        [by_partition(a) for a in (g_pre_mix, g_post_mix, g_pre_ffn, g_post_ffn, g_v, g_out_a, g_out_b)]
        + [conv_mix, conv_ffn], axis=2)
    assert params.shape[2] == NPAR
    b_ada_t = np.asarray(b_ada).reshape(DEPTH * 6 * KD, P).T

    mix_hist = np.asarray(state_conv_mix).reshape(SEQS, DEPTH, 2, HB, P).transpose(1, 4, 3, 0, 2)
    ffn_hist = by_pair(state_conv_ffn, 3).reshape(SEQS, DEPTH, 2, G, 8, P).transpose(1, 3, 5, 4, 0, 2)

    ws = np.asarray(w_spatial)
    w_sp = ws.transpose(0, 3, 1, 2)
    w_sp_s = np.zeros((DEPTH, SEQS * STEP, HA, SEQS, STEP), f)
    for s in range(SEQS):
        w_sp_s[:, s * STEP:(s + 1) * STEP, :, s, :] = ws[:, :, :STEP, :STEP].transpose(0, 3, 1, 2)
    b_sp = np.asarray(b_spatial).reshape(DEPTH, 1, HA * P)

    ada_units = np.asarray(w_ada).reshape(DEPTH, 4, 4, P, ADA_CHUNKS, 512).transpose(0, 4, 1, 3, 2, 5)
    ada_units = np.ascontiguousarray(ada_units).reshape(ADA_TOTAL * 4, P, 4, 512)

    w_units = np.empty((DEPTH * UNITS, P, UNIT), f)
    w_in, w_out, w_up, w_down = (np.asarray(a) for a in (w_in, w_out, w_up, w_down))
    n = 0

    def put(a):
        nonlocal n
        tiles = a.shape[0] // P
        w_units[n] = a.reshape(tiles, P, a.shape[1]).transpose(1, 0, 2).reshape(P, UNIT)
        n += 1

    for l in range(DEPTH):
        def columns(w, first):
            put(w[l, :, first:first + P])

        def down(g):
            for q in range(4):
                put(w_down[l, 512 * g:512 * (g + 1), 512 * q:512 * (q + 1)])

        for j in range(HA):
            columns(w_in, W_A + j * P)
        for j in range(HB):
            for part in (1, 2, 0):
                columns(w_in, 2 * W_A + part * W_B + j * P)
        for j in range(HA):
            columns(w_in, j * P)
        for m in range(KD):
            columns(w_out, m * P)
        for g in range(G):
            for j in range(4):
                for part in range(2):
                    columns(w_up, part * D_FF + (4 * g + j) * P)
                if j == 0 and g:
                    down(g - 1)
        down(G - 1)
    assert n == DEPTH * UNITS

    arrays = {
        "x_t": x_t, "c_t": c_t, "consts": consts, "params": params, "b_ada_t": b_ada_t,
        "mix_hist": mix_hist.reshape(DEPTH, P, -1), "ffn_hist": ffn_hist.reshape(DEPTH, G, P, -1),
        "w_sp": w_sp.reshape(DEPTH, P, -1), "w_sp_s": w_sp_s.reshape(DEPTH, SEQS * STEP, -1), "b_sp": b_sp,
        "ada_units": ada_units, "w_units": w_units,
    }
    arrays = {k: np.ascontiguousarray(v) for k, v in arrays.items()}
    nc = bacc.Bacc("TRN2", target_bir_lowering=False, num_devices=1)
    args = [nc.dram_tensor(k, v.shape, F32, kind="ExternalInput").ap() for k, v in arrays.items()]
    args += [nc.dram_tensor(k, shape, F32, kind="ExternalOutput").ap() for k, shape in _OUTS]
    trunk_kernel(nc, *args)
    r = run_bass_kernel_spmd(nc, [arrays], core_ids=[0]).results[0]

    y = r["y_t"].transpose(2, 1, 0).reshape(T, D_MODEL)
    mix = r["new_mix"].reshape(DEPTH, P, HB, R, 2).transpose(3, 0, 4, 2, 1).reshape(R, DEPTH, 2, W_B)
    ffn = r["new_ffn"].reshape(DEPTH, G, P, 4, 2, R, 2).transpose(5, 0, 6, 4, 1, 3, 2)
    ffn = ffn.reshape(R, DEPTH, 2, 2 * D_FF)
    v = r["v_rows"].transpose(0, 3, 1, 2).reshape(DEPTH, T - P, W_A)
    v_prompt = v[None, :, 0:P]
    v_sample = v[:, P:].reshape(DEPTH, SEQS, STEP, W_A).transpose(1, 0, 2, 3)
    return (y[:SEQ].reshape(1, SEQ, D_MODEL), y[SEQ:].reshape(SEQS, STEP, D_MODEL),
            mix[:1], mix[1:], ffn[:1], ffn[1:], v_prompt, v_sample)
```
